# Optimizing a Trainium2 kernel written in Bass

```python
import jax, jax.numpy as jnp
from jax import lax
import numpy as np

D_MODEL = 1024
BATCH = 1
SEQ = 512
DEPTH = 1
DEC_BATCH = 8
DEC_SEQ = 8
PAST_LEN = 4096
PAGE_SIZE = 128

N_META = 16
HEAD_DIM = 64
FOX_HEADS = 8
RWKV_HEADS = 8
FOX_WIDTH = FOX_HEADS * HEAD_DIM
RWKV_WIDTH = RWKV_HEADS * HEAD_DIM
MIX_WIDTH = FOX_WIDTH + RWKV_WIDTH
DECAY_LORA = 64
ICLR_LORA = 64
GATE_LORA = 128
D_FF = -(-8 * D_MODEL // (3 * 256)) * 256
Q_BLOCK = 128
RMS_EPS = 1e-6
GN_EPS = 64e-5
FOX_COLS = 3 * FOX_WIDTH + FOX_HEADS
RWKV_COLS = 3 * RWKV_WIDTH + DECAY_LORA + ICLR_LORA + GATE_LORA
IN_COLS = FOX_COLS + RWKV_COLS

kernel_name = "fox_rwkv7_hybrid_step"

def rms_norm(x, g):
    x32 = x.astype(jnp.float32)
    y = x32 * lax.rsqrt(jnp.mean(x32 * x32, axis=-1, keepdims=True) + RMS_EPS)
    return (y * g.astype(jnp.float32)).astype(x.dtype)

def fox_attend(q, c_q, segments):
    qf = q.astype(jnp.float32) * (HEAD_DIM ** -0.5)
    cq = jnp.swapaxes(c_q, 1, 2)[..., :, None]
    logits = []
    for k, _, c_k, mask in segments:
        s = jnp.einsum('bqhd,bkhd->bhqk', qf, k.astype(jnp.float32))
        s = s + cq - jnp.swapaxes(c_k, 1, 2)[..., None, :]
        logits.append(jnp.where(mask, s, -jnp.inf))
    p = jax.nn.softmax(jnp.concatenate(logits, axis=-1), axis=-1)
    out = None
    start = 0
    for k, v, _, _ in segments:
        n = k.shape[1]
        o = jnp.einsum('bhqk,bkhd->bqhd', p[..., start:start + n], v.astype(jnp.float32))
        out = o if out is None else out + o
        start += n
    return out

def prompt_fox(q, k, v, logf):
    B, T, H, dh = q.shape
    c = jnp.cumsum(logf, axis=1)
    pos_k = jnp.arange(T)
    meta_mask = pos_k[:N_META][None, :] <= jnp.arange(N_META)[:, None]
    out_meta = fox_attend(q[:, :N_META], c[:, :N_META],
                          ((k[:, :N_META], v[:, :N_META], c[:, :N_META], meta_mask),))

    def block(i):
        start = N_META + i * Q_BLOCK
        q_b = lax.dynamic_slice_in_dim(q, start, Q_BLOCK, axis=1)
        c_b = lax.dynamic_slice_in_dim(c, start, Q_BLOCK, axis=1)
        mask = pos_k[None, :] <= (start + jnp.arange(Q_BLOCK))[:, None]
        return fox_attend(q_b, c_b, ((k, v, c, mask),))

    n_blocks = (T - N_META) // Q_BLOCK
    out = lax.map(block, jnp.arange(n_blocks))
    out = jnp.moveaxis(out, 0, 1).reshape(B, n_blocks * Q_BLOCK, H, dh)
    return jnp.concatenate([out_meta, out], axis=1)

def make_sample_fox(k_past, v_past, logf_past):
    def attn(q, k, v, logf):
        L = q.shape[1]
        P = k_past.shape[1]
        lp = logf_past.astype(jnp.float32)
        r_past = lax.cumsum(lp, axis=1, reverse=True) - lp
        c_new = jnp.cumsum(logf, axis=1)
        past_mask = jnp.ones((L, P), dtype=bool)
        new_mask = jnp.tril(jnp.ones((L, L), dtype=bool))
        return fox_attend(q, c_new, ((k_past, v_past, -r_past, past_mask),
                                     (k, v, c_new, new_mask)))
    return attn

def wkv_step(S, inp):
    r_t, w_t, k_t, v_t, a_t, b_t = inp
    sa = jnp.einsum('bhij,bhj->bhi', S, a_t)
    S = S * w_t[:, :, None, :] + sa[..., None] * b_t[:, :, None, :] + v_t[..., None] * k_t[:, :, None, :]
    y = jnp.einsum('bhij,bhj->bhi', S, r_t)
    return S, y

def rwkv7_time_mix(r, k, v, wl, al, gl, S0, w0, w2, a0, a2, g2, k_k, k_a, r_k, gn_g, gn_b):
    B, T, _ = r.shape
    r, k, v, wl, al, gl = (t.astype(jnp.float32) for t in (r, k, v, wl, al, gl))
    w_log = -jax.nn.softplus(-(w0 + jnp.tanh(wl) @ w2)) - 0.5
    decay = jnp.exp(-jnp.exp(w_log))
    a = jax.nn.sigmoid(a0 + al @ a2)
    g = jax.nn.sigmoid(gl) @ g2
    hd = lambda t: t.reshape(B, T, RWKV_HEADS, HEAD_DIM)
    kk = hd(k * k_k)
    kk = kk / jnp.maximum(jnp.sqrt(jnp.sum(kk * kk, axis=-1, keepdims=True)), 1e-12)
    k = k * (1.0 + (a - 1.0) * k_a)
    r_h, k_h, v_h, w_h, a_h = hd(r), hd(k), hd(v), hd(decay), hd(a)
    xs = tuple(jnp.moveaxis(t, 1, 0) for t in (r_h, w_h, k_h, v_h, -kk, kk * a_h))
    S, y = lax.scan(wkv_step, S0.astype(jnp.float32), xs)
    y = jnp.moveaxis(y, 0, 1)
    mean = jnp.mean(y, axis=-1, keepdims=True)
    var = jnp.mean(jnp.square(y - mean), axis=-1, keepdims=True)
    yn = (y - mean) * lax.rsqrt(var + GN_EPS) * gn_g.reshape(RWKV_HEADS, HEAD_DIM) + gn_b.reshape(RWKV_HEADS, HEAD_DIM)
    bonus = jnp.sum(r_h * k_h * r_k, axis=-1, keepdims=True) * v_h
    out = (yn + bonus).reshape(B, T, RWKV_WIDTH) * g
    return out, S

def trunk_layer(x, shift_prev, wkv_prev, attn_fn, lp):
    (ln1_g, w_in, b_f, mu_shift, w0, w2, a0, a2, g2, k_k, k_a, r_k,
     gn_g, gn_b, w_out, ln2_g, w_gate, w_up, w_down) = lp
    B, T, _ = x.shape
    xn = rms_norm(x, ln1_g)
    x_ext = jnp.concatenate([shift_prev[:, None, :].astype(xn.dtype), xn], axis=1)
    proj = x_ext @ w_in
    fox = proj[:, 1:, :FOX_COLS]
    rw = proj[:, :, FOX_COLS:]
    rw = rw[:, 1:] + (rw[:, :-1] - rw[:, 1:]) * mu_shift
    q, k, v, f = jnp.split(fox, [FOX_WIDTH, 2 * FOX_WIDTH, 3 * FOX_WIDTH], axis=-1)
    logf = jax.nn.log_sigmoid((f + b_f).astype(jnp.float32))
    q = q.reshape(B, T, FOX_HEADS, HEAD_DIM)
    k = k.reshape(B, T, FOX_HEADS, HEAD_DIM)
    v = v.reshape(B, T, FOX_HEADS, HEAD_DIM)
    attn = attn_fn(q, k, v, logf)
    r, kr, vr, wl, al, gl = jnp.split(
        rw, [RWKV_WIDTH, 2 * RWKV_WIDTH, 3 * RWKV_WIDTH, 3 * RWKV_WIDTH + DECAY_LORA,
             3 * RWKV_WIDTH + DECAY_LORA + ICLR_LORA], axis=-1)
    rwkv_out, wkv_new = rwkv7_time_mix(r, kr, vr, wl, al, gl, wkv_prev, w0, w2, a0, a2, g2,
                                       k_k, k_a, r_k, gn_g, gn_b)
    mixed = jnp.concatenate([attn.reshape(B, T, FOX_WIDTH).astype(x.dtype),
                             rwkv_out.astype(x.dtype)], axis=-1) @ w_out
    h = x + mixed
    hn = rms_norm(h, ln2_g)
    h = h + (jax.nn.silu(hn @ w_gate) * (hn @ w_up)) @ w_down
    return h, (k, v, logf.astype(x.dtype), wkv_new.astype(x.dtype), xn[:, -1])

def setup_inputs(seed: int = 0) -> dict:
    key = jax.random.key(seed)
    ks = jax.random.split(key, 40)
    f32 = jnp.float32
    nrm = lambda k, shape, scale: jax.random.normal(k, shape, f32) * scale
    n_pages = PAST_LEN // PAGE_SIZE
    n_pool = (DEC_BATCH * n_pages * 5) // 4
    return {
        "x_prompt": nrm(ks[0], (BATCH, SEQ, D_MODEL), 1.0),
        "x_sample": nrm(ks[1], (DEC_BATCH, DEC_SEQ, D_MODEL), 1.0),
        "cache_k": nrm(ks[2], (DEPTH, n_pool, PAGE_SIZE, FOX_HEADS, HEAD_DIM), 1.0),
        "cache_v": nrm(ks[3], (DEPTH, n_pool, PAGE_SIZE, FOX_HEADS, HEAD_DIM), 1.0),
        "cache_logf": jax.nn.log_sigmoid(9.0 + nrm(ks[4], (DEPTH, n_pool, PAGE_SIZE, FOX_HEADS), 0.5)),
        "state_wkv": nrm(ks[5], (DEPTH, DEC_BATCH, RWKV_HEADS, HEAD_DIM, HEAD_DIM), 0.3),
        "state_shift": nrm(ks[6], (DEPTH, DEC_BATCH, D_MODEL), 1.0),
        "page_table": jax.random.permutation(ks[7], n_pool)[:DEC_BATCH * n_pages].reshape(DEC_BATCH, n_pages).astype(jnp.int32),
        "meta_tokens": nrm(ks[8], (N_META, D_MODEL), 1.0),
        "ln1_g": 1.0 + nrm(ks[9], (DEPTH, D_MODEL), 0.05),
        "w_in": nrm(ks[10], (DEPTH, D_MODEL, IN_COLS), D_MODEL ** -0.5),
        "b_f": 6.0 + nrm(ks[11], (DEPTH, FOX_HEADS), 0.5),
        "mu_shift": jax.random.uniform(ks[12], (DEPTH, RWKV_COLS), f32),
        "w0": jax.random.uniform(ks[13], (DEPTH, RWKV_WIDTH), f32, minval=-6.0, maxval=-1.0),
        "w2": nrm(ks[14], (DEPTH, DECAY_LORA, RWKV_WIDTH), DECAY_LORA ** -0.5),
        "a0": nrm(ks[15], (DEPTH, RWKV_WIDTH), 0.1),
        "a2": nrm(ks[16], (DEPTH, ICLR_LORA, RWKV_WIDTH), ICLR_LORA ** -0.5),
        "g2": nrm(ks[17], (DEPTH, GATE_LORA, RWKV_WIDTH), GATE_LORA ** -0.5),
        "k_k": 0.85 + nrm(ks[18], (DEPTH, RWKV_WIDTH), 0.05),
        "k_a": 1.0 + nrm(ks[19], (DEPTH, RWKV_WIDTH), 0.05),
        "r_k": nrm(ks[20], (DEPTH, RWKV_HEADS, HEAD_DIM), 0.1),
        "gn_g": 1.0 + nrm(ks[21], (DEPTH, RWKV_WIDTH), 0.05),
        "gn_b": nrm(ks[22], (DEPTH, RWKV_WIDTH), 0.02),
        "w_out": nrm(ks[23], (DEPTH, MIX_WIDTH, D_MODEL), MIX_WIDTH ** -0.5),
        "ln2_g": 1.0 + nrm(ks[24], (DEPTH, D_MODEL), 0.05),
        "w_gate": nrm(ks[25], (DEPTH, D_MODEL, D_FF), D_MODEL ** -0.5),
        "w_up": nrm(ks[26], (DEPTH, D_MODEL, D_FF), D_MODEL ** -0.5),
        "w_down": nrm(ks[27], (DEPTH, D_FF, D_MODEL), D_FF ** -0.5),
        "lnf_g": 1.0 + nrm(ks[28], (D_MODEL,), 0.05),
    }

def reference(x_prompt, x_sample, cache_k, cache_v, cache_logf, state_wkv, state_shift, page_table,
              meta_tokens, ln1_g, w_in, b_f, mu_shift, w0, w2, a0, a2, g2, k_k, k_a, r_k,
              gn_g, gn_b, w_out, ln2_g, w_gate, w_up, w_down, lnf_g):
    B = x_prompt.shape[0]
    DB = x_sample.shape[0]
    n_pages = PAST_LEN // PAGE_SIZE
    xp = jnp.concatenate([jnp.broadcast_to(meta_tokens[None].astype(x_prompt.dtype), (B, N_META, D_MODEL)),
                          x_prompt], axis=1)
    xs = x_sample
    p_states = []
    s_states = []
    for l in range(DEPTH):
        lp = (ln1_g[l], w_in[l], b_f[l], mu_shift[l], w0[l], w2[l], a0[l], a2[l], g2[l], k_k[l], k_a[l],
              r_k[l], gn_g[l], gn_b[l], w_out[l], ln2_g[l], w_gate[l], w_up[l], w_down[l])
        xp, st_p = trunk_layer(xp, jnp.zeros((B, D_MODEL), xp.dtype),
                               jnp.zeros((B, RWKV_HEADS, HEAD_DIM, HEAD_DIM), jnp.float32),
                               prompt_fox, lp)
        k_past = cache_k[l][page_table].reshape(DB, n_pages * PAGE_SIZE, FOX_HEADS, HEAD_DIM)
        v_past = cache_v[l][page_table].reshape(DB, n_pages * PAGE_SIZE, FOX_HEADS, HEAD_DIM)
        logf_past = cache_logf[l][page_table].reshape(DB, n_pages * PAGE_SIZE, FOX_HEADS)
        xs, st_s = trunk_layer(xs, state_shift[l], state_wkv[l],
                               make_sample_fox(k_past, v_past, logf_past), lp)
        p_states.append(st_p)
        s_states.append(st_s)
    y_prompt = rms_norm(xp[:, N_META:], lnf_g)
    y_sample = rms_norm(xs, lnf_g)
    k_prompt = jnp.stack([s[0] for s in p_states])
    v_prompt = jnp.stack([s[1] for s in p_states])
    logf_prompt = jnp.stack([s[2] for s in p_states])
    wkv_prompt = jnp.stack([s[3] for s in p_states])
    shift_prompt = jnp.stack([s[4] for s in p_states])
    k_sample = jnp.stack([s[0] for s in s_states])
    v_sample = jnp.stack([s[1] for s in s_states])
    logf_sample = jnp.stack([s[2] for s in s_states])
    wkv_sample = jnp.stack([s[3] for s in s_states])
    shift_sample = jnp.stack([s[4] for s in s_states])
    return (y_prompt, y_sample, k_prompt, v_prompt, logf_prompt, wkv_prompt, shift_prompt,
            k_sample, v_sample, logf_sample, wkv_sample, shift_sample)


_drawn_inputs = setup_inputs


def setup_inputs(seed=0):
    import zlib

    import numpy as np

    out = dict(_drawn_inputs(seed))
    spreads = {}
    factors = {'cache_k': 3.694, 'cache_v': 2.939, 'cache_logf': 200.0, 'gn_g': 2.985, 'gn_b': 7.004}
    for name, (base, spread) in spreads.items():
        noise = np.random.default_rng([zlib.crc32(name.encode()), seed]).standard_normal(out[name].shape)
        drawn = base * np.exp(spread * noise) if base else spread * noise
        out[name] = __import__('jax').numpy.asarray(drawn.astype(out[name].dtype))
    for name, factor in factors.items():
        out[name] = (out[name] * factor).astype(out[name].dtype)
    return out
```

```python
from contextlib import ExitStack

import concourse.bass as bass
from concourse import mybir

F32 = mybir.dt.float32
I32 = mybir.dt.int32
ALU = mybir.AluOpType
ACT = mybir.ActivationFunctionType
AX = mybir.AxisListType

P = 128
D = 1024
KT = D // P
NMETA = 16
SEQ = 512
NPT = NMETA + SEQ
DB = 8
DS = 8
NS = DB * DS
H = 8
HD = 64
NG = H * HD // P
FOXW = H * HD
FOXC = 3 * FOXW + H
DFF = 2816
NF = DFF // P
NTILE = 5
RAW = 602
RS0 = 1 + NPT
TL = NTILE * P
OUTC = SEQ + NS
PAGE = 128
NPG = 32
NB = 512
NEG = -1.0e30
RMS_EPS = 1e-6
GN_EPS = 64e-5
E_HALF = 0.6065306597126334
PAR_ROWS = [("ln1_g", 8), ("mu_shift", 14), ("w0", 4), ("a0", 4), ("k_k", 4), ("k_a", 4), ("r_k", 4), ("gn_g", 4),
            ("gn_b", 4), ("ln2_g", 8)]
NPAR = sum(n for _, n in PAR_ROWS)


class Chain:

    def __init__(self, eng, sem):
        self.eng, self.sem, self.n = eng, sem, 0

    def __call__(self, ins):
        ins.then_inc(self.sem, 1)
        self.n += 1
        return ins

    def wait(self):
        self.eng.wait_ge(self.sem, self.n)


def build(nc, t_in, t_out):
    ctx = ExitStack()
    with ctx:
        def sem(name):
            return ctx.enter_context(nc.semaphore(name))

        arena = ctx.enter_context(nc.sbuf_tensor("arena", [P, 52800], F32))
        PS = ctx.enter_context(nc.psum_tensor("PS", [P, 8, NB], F32))
        ptab = ctx.enter_context(nc.sbuf_tensor("ptab", [1, DB * NPG], I32))
        top = [0]

        def at(off, *dims):
            n = 1
            for d in dims:
                n *= d
            v = arena[:, off:off + n]
            if len(dims) == 2:
                v = v.rearrange("p (a b) -> p a b", a=dims[0])
            elif len(dims) == 3:
                v = v.rearrange("p (a b c) -> p a b c", a=dims[0], b=dims[1])
            elif len(dims) == 4:
                v = v.rearrange("p (a b c d) -> p a b c d", a=dims[0], b=dims[1], c=dims[2])
            return v

        def new(*dims):
            n = 1
            for d in dims:
                n *= d
            off = top[0]
            top[0] += n
            assert top[0] <= 52800, top[0]
            return at(off, *dims)

        ident = new(P)
        ones = new(P)
        headones = new(P)
        sel = new(H, P)
        causal = new(P)
        level = new(6, P)
        up_incl = new(2, P)
        up_strict = new(2, P)
        low_strict = new(2, P)
        later_page = new(P)
        later_key = new(P)
        chunk_mask = new(TL)
        forget_mask = new(RAW)
        par = new(NPAR)
        ss, rstd = new(NTILE), new(NTILE)
        bf_col = new(1)
        small = new(8)
        RN = new(DB, H, DS)
        cnat = new(H)
        seq_of = new(DB)
        Dc = new(NG, 1 + DB + SEQ // 64)
        kTS = new(NG, P)
        lognat = new(NTILE, H)
        QB = new(DB, NG, 16)
        MIX0 = top[0]
        mixT = new(2 * NG, OUTC)
        qT_off = top[0]
        kT = new(NG, RAW)
        qT = new(NG, RAW)
        vnat = new(NTILE, FOXW)
        FREE = top[0]
        x = new(NTILE, D)
        B0 = top[0]

        pcol = {}
        at_row = 0
        for name, n in PAR_ROWS:
            pcol[name] = at_row
            at_row += n

        def pc(name, i, lo=0, hi=P):
            return par[lo:hi, pcol[name] + i:pcol[name] + i + 1]

        top[0] = B0
        xnT = new(KT, RAW)
        wring = new(2, KT, 520)
        XR = new(14, TL)
        xs = at(MIX0, 2, D)
        xsq = at(MIX0 + 2 * D, D)
        raw = new(2, RAW)
        diff = new(RAW)
        parn = at(MIX0 + 3 * D, P)
        kn = new(NTILE, FOXW)
        fT = new(RAW)
        f2 = at(MIX0 + 3 * D + P, RAW)
        xnS = at(MIX0 + 3 * D + P + RAW, KT, NS)
        assert 3 * D + P + RAW + KT * NS <= 2 * NG * OUTC
        cT = new(RAW)
        LT = new(TL)
        shn = new(D)
        END1 = top[0]

        top[0] = B0
        NCB = new(H, NPT)
        Sp = new(2, 544)
        PT = new(2, NTILE, P)
        mxp, nmp, smp, rcp = new(2), new(2), new(2), new(2)
        assert top[0] <= B0 + KT * RAW + 2 * KT * 520

        names = """consts x0_zeroed par_in par_turned par_ready square_done var_done std_done rstd_done xs_ready xT_turned
        xnT_ready w_landed0 w_landed1 proj_ready proj_taken nat_ready nat_taken mixed_done f_in logf_a logf_v log_ready
        ncb_ready ncb_taken s_ready s_added mx_ready exp_done p_ready pt_ready pt_taken pv_ready o_taken out_done
        qb_ready kts_ready act_c dve_c pool_c pt_zero shn_turned shn_ready
        lr_in lr_act lr_ready lr_taken hs_in hs_ready hs_taken pre_done L_ready decays root_in root_done
        turned turned_taken gram_b gram_b_taken gram_m gram_k gram_k_taken g_first x_turned x_taken r_ready r_taken g_ready g_added
        nv_ready nv_taken wt_ready wt_taken st_done u_ready u_taken st_ready s0_in0 s0_in1 s0_turned s0_taken ut_ready ut_taken
        us_ready us_taken y_ready y_taken um_ready um_used sn_ready sn_taken so_turned so_taken so_out0 so_out1 fs_turned
        fs_taken fs_out yc_ready rwkv_done prev_tile
        ptab_in k_free v_free attn_done wo_in lnf_in gu_ready down_used pidx_in ln_in y_final lt_turned lt_taken tu_ready
        r_sums rl_taken kt_taken sc_taken sc_page new_ready new_taken mx_in mx_turned dg_ready mx_spread
        sm_ready sum_ready exp_out mixed_out h_ready act_ready down_tile down_taken p_in
        silu_done rden_done m1_done o_done""".split()
        S = {n: sem(n) for n in names}
        X0 = FREE
        WA = at(X0, FOXW)
        G2 = at(X0 + FOXW, FOXW)
        MtRb = at(X0, H, 2, P)
        NtRk = at(X0 + 2048, H, 2, P)
        Ms = at(X0 + 4096, H, P)
        AR = at(B0, 2, NG, TL)
        Kd = at(B0 + 5120, NG, TL)
        Bd = at(B0 + 7680, NG, TL)
        gate = at(B0 + 10240, NG, TL)
        assert 12800 <= KT * RAW + 2 * KT * 520
        XR0 = B0 + KT * RAW + 2 * KT * 520
        HI = XR0 + 14 * TL
        kk = at(HI, NG, TL)
        T2 = at(HI + 2560, NG, TL)
        nat_ = at(HI + 2560, 4, FOXW)
        Xs = at(HI + 2560 + 2048, H, P)
        NVs = at(HI + 2560 + 3072, FOXW)
        Wt = at(HI + 2560 + 3584, NG, P)
        Us = at(HI + 2560 + 4096, FOXW)
        assert HI + 2560 + 4608 <= 52800, HI
        YT = at(XR0, NG, TL)
        S0n = at(XR0 + 2560, DB // 2, NG, P)
        ST = at(XR0 + 2560 + 2048, NG, P)
        Rs = at(XR0 + 12 * TL, H, P)
        S0T = at(qT_off, DB, NG, P)
        tmpS = at(qT_off + 4096, NG, HD)
        Sn = S0n.rearrange("p a b c -> p (a b c)").rearrange("p (g n) -> p g n", g=NG)
        SOo = at(X0 + 2048, 2, DB, P)
        Um = at(X0, 2, DB, HD)
        UTs = Rs.rearrange("p a b -> p (a b)")[:, 0:NG * NS].rearrange("p (g n) -> p g n", g=NG)
        NRING = 16
        LOT = 4
        top[0] = B0
        Kr = new(NRING, FOXW)
        Vr = new(NRING, FOXW)
        KTs = new(2, NG, P)
        Sb = new(NPG + 1, H * DS)
        Pb = new(NPG + 1, H * DS)
        Rl = new(DB, H, NPG)
        Ln = new(2, PAGE * H)
        mx, dg, sm, rden = new(P), new(64), new(64), new(64)
        m1 = new(1)
        tot = new(2, H)
        pidx = new(2).bitcast(I32)
        LTk = Sb.rearrange("p a b -> p (a b)")[:, 0:2048].rearrange("p (t h n) -> p t h n", t=2, h=H)
        TU = Pb.rearrange("p a b -> p (a b)")[:, 0:2048].rearrange("p (t h n) -> p t h n", t=2, h=H)
        assert top[0] <= 52800
        hT = at(qT_off, KT, OUTC)
        sgate = at(qT_off + KT * OUTC, 2, OUTC)
        lnf = at(qT_off + KT * OUTC + 2 * OUTC, D)
        assert KT * OUTC + 2 * OUTC + D <= X0 - qT_off
        top[0] = B0
        FR = 3
        fring = new(FR, 4096)
        FF0 = top[0]
        actT = new(NF, OUTC)
        xs2 = new(2, D)
        xsq2 = new(D)
        wo = at(FF0, KT, D)
        assert top[0] <= 52800
        x_in = [sem(f"x_in{i}") for i in range(NTILE)]

        k_in = [sem(f"k_in{i}") for i in range(NRING // LOT)]
        v_in = [sem(f"v_in{i}") for i in range(NRING // LOT)]
        f_in = [sem(f"f_in{i}") for i in range(FR)]
        block = ctx.enter_context(nc.Block())

        WCH = [(0, 512), (512, 512), (1024, 520), (1544, 512), (2056, 512), (2568, 512), (3080, 256)]
        w_in = t_in["w_in"]
        ITEMS = [(0, g * P, P, ("q", g)) for g in range(NG)] + [(1, g * P, P, ("k", g)) for g in range(NG)] + \
            [(2, 512, H, ("f", 0))] + \
            [(3 + c, g * P, P, ("rw", 4 * c + g)) for c in range(3) for g in range(NG)] + \
            [(6, 0, P, ("rw", 12)), (6, P, P, ("rw", 13))]
        HALF = RAW // 2
        NRW0 = 9
        N_OUT_DMA = [0]
        N_FIRST_OUT = 11

        def samp(v, first):
            return v[:, RS0:RS0 + 9 * DB].rearrange("p (b n) -> p b n", n=9)[:, :, first:first + DS]

        def samps(v):
            return v[:, :, RS0:RS0 + 9 * DB].rearrange("p k (b n) -> p k b n", n=9)[:, :, :, 1:9]

        def out_dma(eng, dst, src):
            N_OUT_DMA[0] += 1
            eng.dma_start(dst, src).then_inc(S["out_done"], 16)

        @block.sync
        def _(sp):
            for name, n in PAR_ROWS:
                src = t_in[name]
                if name == "r_k":
                    src = src[0].rearrange("h d -> (h d)").rearrange("(a p) -> a p", p=P)
                elif name in ("lnf_g",):
                    src = src.rearrange("(a p) -> a p", p=P)
                else:
                    src = src[0].rearrange("(a p) -> a p", p=P)
                r = pcol[name]
                sp.dma_start(parn[r:r + n, :], src).then_inc(S["par_in"], 16)
            sp.dma_start(bf_col[0:H, :], t_in["b_f"].rearrange("o h -> h o")).then_inc(S["f_in"], 16)
            sp.wait_ge(S["x0_zeroed"], 1)
            sp.dma_start(x[0:NMETA, 0, :], t_in["meta_tokens"]).then_inc(x_in[0], 16)
            sp.dma_start(x[32:32 + DB, 0, :], t_in["state_shift"][0]).then_inc(x_in[0], 16)
            sp.dma_start(x[64:P, 0, :], t_in["x_sample"].rearrange("b t d -> (b t) d")).then_inc(x_in[0], 16)
            for i in range(1, NTILE):
                sp.dma_start(x[:, i, :], t_in["x_prompt"][0, (i - 1) * P:i * P, :]).then_inc(x_in[i], 16)
            for c, (c0, n) in enumerate(WCH):
                if c >= 2:
                    sp.wait_ge(S["proj_ready"], sum(1 for it in ITEMS if it[0] <= c - 2))
                    if c - 2 == 2:
                        sp.wait_ge(S["nat_ready"], NTILE)
                sp.dma_start(wring[:, c % 2, :, 0:n],
                             w_in[0].rearrange("(k p) n -> p k n", p=P)[:, :, c0:c0 + n]).then_inc(S[f"w_landed{c % 2}"], 16)

            sp.wait_ge(S["xs_ready"], NTILE)
            sp.dma_start(WA[0:64, :], t_in["w2"][0]).then_inc(S["lr_in"], 16)
            sp.dma_start(WA[64:P, :], t_in["a2"][0]).then_inc(S["lr_in"], 16)
            sp.dma_start(G2, t_in["g2"][0]).then_inc(S["lr_in"], 16)
            sp.wait_ge(S["pre_done"], 1)
            for b in range(DB):
                if b == DB // 2:
                    sp.wait_ge(S["s0_turned"], DB // 2)
                for hp in range(2):
                    lo = slice(64 * hp, 64 * hp + 64)
                    src = t_in["state_wkv"][0, b].rearrange("(g a) i j -> a i g j", a=2)[hp]
                    sp.dma_start(S0n[lo, b % (DB // 2), :, lo], src).then_inc(S[f"s0_in{2 * b // DB}"], 16)
            sp.dma_start(ptab[:, :], t_in["page_table"].rearrange("b p -> (b p)").unsqueeze(0)).then_inc(S["ptab_in"], 16)
            sp.wait_ge(S["ptab_in"], 16)
            sp.wait_ge(S["rwkv_done"], 1)
            n_pool = t_in["cache_k"].shape[1]
            k_pages = t_in["cache_k"][0].rearrange("n p h d -> n p (h d)")
            v_pages = t_in["cache_v"][0].rearrange("n p h d -> n p (h d)")

            def load_page(pages, ring, free, landed, b, p):
                sp.wait_ge(S[free], b * NPG + (p + 1))
                page = sp.value_load(ptab[0:1, bass.ds(b * NPG + p, 1)], min_val=0, max_val=n_pool - 1)
                sp.dma_start(ring[:, p % NRING, :], pages[bass.ds(page, 1)].rearrange("o p n -> p (o n)"))\
                    .then_inc(landed[p % NRING // LOT], 16)

            for p in range(NPG):
                load_page(k_pages, Kr, "k_free", k_in, 0, p)
            with sp.Fori(1, DB) as b:
                for p in range(NPG):
                    load_page(k_pages, Kr, "k_free", k_in, b, p)
                    load_page(v_pages, Vr, "v_free", v_in, b - 1, p)
            for p in range(NPG):
                load_page(v_pages, Vr, "v_free", v_in, DB - 1, p)
            sp.dma_start(x[64:P, 0, :], t_in["x_sample"].rearrange("b t d -> (b t) d")).then_inc(x_in[0], 16)
            for i in range(1, NTILE):
                sp.dma_start(x[:, i, :], t_in["x_prompt"][0, (i - 1) * P:i * P, :]).then_inc(x_in[i], 16)
            sp.wait_ge(S["attn_done"], 1)
            sp.dma_start(wo, t_in["w_out"][0].rearrange("(k p) n -> p k n", p=P)).then_inc(S["wo_in"], 16)
            sp.dma_start(lnf, t_in["lnf_g"].partition_broadcast(P)).then_inc(S["lnf_in"], 16)
            for r in range(17):
                slot = fring[:, r % FR, :]
                if r >= FR:
                    if r - FR < 11:
                        sp.wait_ge(S["gu_ready"], 2 * (r - FR + 1))
                    else:
                        sp.wait_ge(S["down_used"], r - FR - 10)
                if r < 11:
                    for w, name in enumerate(("w_gate", "w_up")):
                        sp.dma_start(slot[:, w * 2048:(w + 1) * 2048].rearrange("p (k n) -> p k n", k=KT),
                                     t_in[name][0].rearrange("(k p) n -> p k n", p=P)[:, :, r * 256:(r + 1) * 256])\
                            .then_inc(f_in[r % FR], 16)
                else:
                    half, c = (r - 11) // 3, (r - 11) % 3
                    n0, n1 = 8 * c, min(8 * c + 8, NF)
                    sp.dma_start(slot[:, 0:(n1 - n0) * NB].rearrange("p (k n) -> p k n", n=NB),
                                 t_in["w_down"][0].rearrange("(k p) n -> p k n", p=P)[:, n0:n1, half * NB:(half + 1) * NB])\
                        .then_inc(f_in[r % FR], 32)

        @block.gpsimd
        def _(pool):
            chain = Chain(pool, S["pool_c"])
            g = nc.gpsimd
            g.memset(x[:, 0, :], 0.0).then_inc(S["x0_zeroed"], 1)
            pool.wait_ge(S["x0_zeroed"], 1)

            def ch(ins):
                chain(ins)
                chain.wait()

            def keep(v, pattern, base, cm, fill=0.0):
                ch(g.affine_select(out=v, in_=v, compare_op=ALU.is_ge, fill=fill, base=base, pattern=pattern,
                                   channel_multiplier=cm))

            ch(g.memset(ident, 0.0))
            ch(g.affine_select(out=ident, in_=ident, compare_op=ALU.not_equal, fill=1.0, base=0, pattern=[[-1, P]],
                               channel_multiplier=1))
            ch(g.memset(ones, 1.0))
            ch(g.memset(headones, 0.0))
            for q in range(2):
                ch(g.memset(headones[64 * q:64 * q + 64, 64 * q:64 * q + 64], 1.0))
            ch(g.memset(sel, 0.0))
            ch(g.affine_select(out=sel, in_=sel, compare_op=ALU.not_equal, fill=1.0, base=0, pattern=[[-1, H], [0, P]],
                               channel_multiplier=1))
            ch(g.memset(causal, 0.0))
            keep(causal, [[-1, P]], 0, 1, NEG)
            ch(g.memset(level, 0.0))
            for l in range(6):
                n = 2 << l
                v = level[:, l, :].rearrange("p (a c) -> p a c", c=n)[:, :, n // 2:n]
                ch(g.memset(v, 1.0))
                keep(v, [[-n, P // n], [0, n // 2]], 0, 1)
                keep(v, [[n, P // n], [0, n // 2]], n // 2 - 1, -1)
            for kind in range(2):
                for m, off in ((up_incl, 0), (up_strict, -1)):
                    v = m[:, kind, :]
                    ch(g.memset(v, 1.0))
                    keep(v, [[1, P]], off, -1)
                    keep(v, [[-64, 2], [0, 64]], 0, 1)
                    if kind == 0:
                        keep(v[:, 64:P], [[-DS, DB], [0, DS]], -64, 1)
                v = low_strict[:, kind, :]
                ch(g.memset(v, 1.0))
                keep(v, [[-1, P]], -1, 1)
                keep(v, [[64, 2], [0, 64]], 63, -1)
                if kind == 0:
                    keep(v[:, 64:P], [[DS, DB], [0, DS]], 64 + DS - 1, -1)
            for v, n in ((later_page, NPG), (later_key, P)):
                ch(g.memset(v, 1.0))
                keep(v, [[-1, P]], -1, 1)
                if n < P:
                    keep(v, [[n, P // n], [0, n]], n - 1, -1)
            ch(g.memset(chunk_mask, 1.0))
            ch(g.memset(forget_mask, 1.0))
            ch(g.memset(chunk_mask[:, 0:1], 0.0))
            ch(g.memset(chunk_mask[:, 64:P].rearrange("p (b t) -> p b t", t=DS)[:, :, 0:1], 0.0))
            ch(g.memset(chunk_mask[:, P:TL].rearrange("p (c t) -> p c t", t=64)[:, :, 0:1], 0.0))
            ch(g.memset(forget_mask[:, 0:2], 0.0))
            ch(g.memset(forget_mask[:, RS0:RS0 + 9 * DB].rearrange("p (b n) -> p b n", n=9)[:, :, 0:2], 0.0))
            ch(g.memset(RN, 0.0))
            keep(RN, [[-DS, DB], [0, H], [0, DS]], -64, 1, NEG)
            keep(RN, [[DS, DB], [0, H], [1, DS]], 64, -1, NEG)
            ch(g.memset(seq_of, 1.0))
            keep(seq_of, [[-DS, DB]], -64, 1)
            keep(seq_of, [[DS, DB]], 64 + DS - 1, -1)
            ch(g.memset(xnT[:, :, 0:1], 0.0))
            ch(g.memset(xnT[:, :, RAW - 1:RAW], 0.0))
            ch(g.memset(XR, 0.0))
            ch(g.memset(vnat[:, 0, :], 0.0))
            ch(g.memset(LT, 0.0))
            ch(g.memset(QB, 0.0))
            ch(g.memset(kTS[:, :, 0:64], 0.0))
            g.memset(small, 0.0).then_inc(S["consts"], 1)
            k_out, v_out = t_out["k_prompt"][0, 0], t_out["v_prompt"][0, 0]
            pool.wait_ge(S["nat_taken"], 12)
            flat = "t h d -> t (h d)"
            for dst, src in ((k_out, kn), (v_out, vnat)):
                dst = dst.rearrange(flat)
                out_dma(pool, dst[0:NMETA, :], src[0:NMETA, 0, :])
                out_dma(pool, dst[NMETA:NPT, :].rearrange("(i p) n -> p i n", p=P), src[:, 1:5, :])
            out_dma(pool, t_out["k_sample"][0].rearrange("b t h d -> (b t) (h d)"), kn[64:P, 0, :])
            out_dma(pool, t_out["v_sample"][0].rearrange("b t h d -> (b t) (h d)"), vnat[64:P, 0, :])
            lf = t_out["logf_prompt"][0, 0]
            out_dma(pool, lf[0:NMETA, :], lognat[0:NMETA, 0, :])
            out_dma(pool, lf[NMETA:NPT, :].rearrange("(i p) n -> p i n", p=P), lognat[:, 1:5, :])
            out_dma(pool, t_out["logf_sample"][0].rearrange("b t h -> (b t) h"), lognat[64:P, 0, :])
            pool.wait_ge(S["shn_ready"], 1)
            out_dma(pool, t_out["shift_prompt"][0], shn[0:1, :])
            out_dma(pool, t_out["shift_sample"][0], shn[1:1 + DB, :])
            w_out_ = t_out["wkv_sample"][0]
            for g in range(NG):
                pool.wait_ge(S["so_taken"], g + 1)
                for hp in range(2):
                    N_OUT_DMA[0] += 0
                    pool.dma_start(w_out_[:, 2 * g + hp].rearrange("b i j -> i b j"), SOo[0:64, g % 2, :, 64 * hp:64 * hp + 64])\
                        .then_inc(S[f"so_out{g % 2}"], 16)
            pool.wait_ge(S["fs_taken"], 1)
            wp = t_out["wkv_prompt"][0, 0].rearrange("(g a) i j -> a i g j", a=2)
            for hp in range(2):
                lo = slice(64 * hp, 64 * hp + 64)
                pool.dma_start(wp[hp], Xs[lo, 0:NG, lo]).then_inc(S["fs_out"], 16)
            pool.wait_ge(S["rwkv_done"], 1)
            pool.wait_ge(S["v_free"], NRING)
            with nc.allow_non_contiguous_dma(reason="256 page numbers"):
                pool.dma_start(pidx, t_in["page_table"].rearrange("(t b) p -> (b p) t", t=2)).then_inc(S["pidx_in"], 16)
            pool.wait_ge(S["pidx_in"], 16)
            for t in range(2):
                nc.gpsimd.indirect_dma_start(
                    Ln[:, t, :], None, t_in["cache_logf"][0].rearrange("n p h -> n (p h)"),
                    bass.IndirectOffsetOnAxis(pidx[:, t:t + 1], 0)).then_inc(S["ln_in"], 16)
            for n, i in enumerate([1, 2, 3, 4, 0]):
                pool.wait_ge(S["y_final"], n + 1)
                if i == 0:
                    out_dma(pool, t_out["y_sample"].rearrange("b t d -> (b t) d"), x[64:P, 0, :])
                else:
                    out_dma(pool, t_out["y_prompt"][0, (i - 1) * P:i * P, :], x[:, i, :])

        @block.tensor
        def _(pe):
            mm = nc.tensor.matmul
            tr = nc.tensor.transpose
            pe.wait_ge(S["consts"], 1)
            pe.wait_ge(S["par_in"], 16 * len(PAR_ROWS))
            tr(PS[:, 7, 0:NPAR], parn[0:NPAR, :], ident[0:NPAR, 0:NPAR]).then_inc(S["par_turned"], 1)
            for i in range(NTILE):
                pe.wait_ge(S["xs_ready"], i + 1)
                if i >= 2:
                    pe.wait_ge(S["xnT_ready"], i - 1)
                for f in range(KT):
                    ins = tr(PS[:, 2 * (i % 2) + f // 4, (f % 4) * P:(f % 4 + 1) * P], xs[:, i % 2, f * P:(f + 1) * P], ident)
                ins.then_inc(S["xT_turned"], 1)
            pe.wait_ge(S["xnT_ready"], NTILE)
            pe.wait_ge(S["par_ready"], 1)

            nat = [0]

            def nat_slot():
                n = nat[0]
                if n >= 2:
                    pe.wait_ge(S["nat_taken"], n - 1)
                nat[0] += 1
                return PS[:, 6 + n % 2, :]

            def k_rows():
                pe.wait_ge(S["proj_taken"], 2 * NG)
                pe.wait_ge(S["kts_ready"], 1)
                for j in range(6):
                    o = nat_slot()
                    n = (NMETA, P, P, P, P, NS)[j]
                    for g in range(NG):
                        src = kT[:, g, 1:1 + NMETA] if j == 0 else kTS[:, g, 64:P] if j == 5 else \
                            kT[:, g, 17 + P * (j - 1):17 + P * j]
                        ins = tr(o[0:n, g * P:(g + 1) * P], src, ident)
                    ins.then_inc(S["nat_ready"], 1)

            def v_rows():
                for i in range(NTILE):
                    o = nat_slot()
                    parts = [(o, 17 + P * (i - 1), P)] if i else [(o[0:NMETA], 1, NMETA), (o[64:P], None, NS)]
                    for dst, c0, n in parts:
                        for k in range(KT):
                            src = xnS[:, k, :] if c0 is None else xnT[:, k, c0:c0 + n]
                            ins = mm(dst, src, wring[:, 0, k, 0:FOXW], start=(k == 0), stop=(k == KT - 1))
                    ins.then_inc(S["nat_ready"], 1)

            for f in range(KT):
                ins = tr(PS[0:9, f // 4 * 1 + 4, (f % 4) * P:(f % 4 + 1) * P], xnT[:, f, 528:601:9], ident)
            ins.then_inc(S["shn_turned"], 1)
            seen = -1
            for n, (c, c0, width, dest) in enumerate(ITEMS):
                if c != seen:
                    seen = c
                    pe.wait_ge(S[f"w_landed{c % 2}"], 16 * (c // 2 + 1))
                if n == 2:
                    pe.wait_ge(S["shn_ready"], 1)
                if n >= 3:
                    pe.wait_ge(S["proj_taken"], n - 2)
                for half in range(2):
                    for k in range(KT):
                        ins = mm(PS[0:width, 2 * (n % 3) + half, 0:HALF], wring[:, c % 2, k, c0:c0 + width],
                                 xnT[:, k, half * HALF:(half + 1) * HALF], start=(k == 0), stop=(k == KT - 1))
                ins.then_inc(S["proj_ready"], 1)
                if dest[0] == "f":
                    v_rows()
                    k_rows()
            pe.wait_ge(S["log_ready"], 1)
            o = nat_slot()
            for i in range(NTILE):
                tr(o[:, i * H:(i + 1) * H], LT[0:H, i * P:(i + 1) * P], ident[0:H, 0:H])
            tr(o[:, NTILE * H:(NTILE + 1) * H], f2[0:H, 0:P], ident[0:H, 0:H]).then_inc(S["nat_ready"], 1)

            pe.wait_ge(S["proj_taken"], len(ITEMS))
            for h in range(H):
                if h >= 3:
                    pe.wait_ge(S["ncb_taken"], h - 2)
                for half in range(2):
                    ins = mm(PS[:, 2 * (h % 3) + half, 0:NPT // 2], sel[0:H, h, :],
                             cT[0:H, 1 + half * (NPT // 2):1 + (half + 1) * (NPT // 2)], start=True, stop=True)
                ins.then_inc(S["ncb_ready"], 1)
            pe.wait_ge(S["ncb_taken"], H)
            pe.wait_ge(S["nat_taken"], 12)
            pe.wait_ge(S["pt_zero"], 1)

            def scores(n):
                g, i, hp = n // 8, n // 2 % 4, n % 2
                if n >= 2:
                    pe.wait_ge(S["s_added"], n - 1)
                nk = (NMETA + P * (i + 1)) // 2
                lo = 64 * hp
                for half in range(2):
                    ins = mm(PS[:, 2 * hp + half, 0:nk], qT[lo:lo + 64, g, 17 + P * i:17 + P * (i + 1)],
                             kT[lo:lo + 64, g, 1 + half * nk:1 + (half + 1) * nk], start=True, stop=True)
                ins.then_inc(S["s_ready"], 1)

            def turn_probs(n):
                i = n // 2 % 4
                pe.wait_ge(S["p_ready"], n + 1)
                if n >= 1:
                    pe.wait_ge(S["pt_taken"], n)
                tr(PS[0:NMETA, 5, 0:P], Sp[:, n % 2, 0:NMETA], ident)
                for kt in range(i + 1):
                    ins = tr(PS[:, 4, kt * P:(kt + 1) * P], Sp[:, n % 2, NMETA + kt * P:NMETA + (kt + 1) * P], ident)
                ins.then_inc(S["pt_ready"], 1)

            def weigh_values(n):
                g, i, hp = n // 8, n // 2 % 4, n % 2
                it = n // 2
                pe.wait_ge(S["pt_taken"], n + 1)
                if it >= 2 and hp == 0:
                    pe.wait_ge(S["o_taken"], it - 1)
                vc = slice((2 * g + hp) * HD, (2 * g + hp + 1) * HD)
                o = PS[64 * hp:64 * hp + 64, 6 + it % 2, 0:P]
                for kt in range(i + 1):
                    mm(o, vnat[:, 1 + kt, vc], PT[:, n % 2, kt, :], start=(kt == 0), stop=False)
                mm(o, vnat[:, 0, vc], PT[:, n % 2, 4, :], start=False, stop=True).then_inc(S["pv_ready"], 1)

            scores(0)
            for n in range(32):
                if n + 1 < 32:
                    scores(n + 1)
                turn_probs(n)
                if n >= 1:
                    weigh_values(n - 1)
            weigh_values(31)

            pe.wait_ge(S["o_taken"], 16)
            pe.wait_ge(S["lr_in"], 48)
            pe.wait_ge(S["lr_act"], 2)
            HT = TL // 2
            for j in range(12):
                g = j % 4
                if j >= 3:
                    pe.wait_ge(S["lr_taken"], j - 2)
                for half in range(2):
                    c = slice(half * HT, (half + 1) * HT)
                    o = PS[:, 2 * (j % 3) + half, 0:HT]
                    w = slice(g * P, (g + 1) * P)
                    if j < 4:
                        ins = mm(o, WA[0:64, w], XR[0:64, 12, c], start=True, stop=True)
                    elif j < 8:
                        ins = mm(o, WA[64:P, w], XR[64:P, 12, c], start=True, stop=True)
                    else:
                        ins = mm(o, G2[:, w], XR[:, 13, c], start=True, stop=True)
                ins.then_inc(S["lr_ready"], 1)
            pe.wait_ge(S["lr_taken"], 12)

            def head_sums(src, turn):
                pe.wait_ge(S["hs_in"], turn)
                for g in range(NG):
                    n = 4 * (turn - 1) + g
                    if n >= 3:
                        pe.wait_ge(S["hs_taken"], n - 2)
                    for half in range(2):
                        ins = mm(PS[:, 2 * (n % 3) + half, 0:HT], headones, src[:, g, half * HT:(half + 1) * HT],
                                 start=True, stop=True)
                    ins.then_inc(S["hs_ready"], 1)

            head_sums(T2, 1)
            head_sums(T2, 2)
            pe.wait_ge(S["hs_taken"], 8)
            pe.wait_ge(S["pre_done"], 1)

            for t in range(NTILE):
                c0 = t * P
                tile = slice(c0, c0 + P)
                nlev = 3 if t == 0 else 5
                lev0 = 0 if t == 0 else 3 + 5 * (t - 1)
                ch0 = 0 if t == 0 else 1 + 2 * (t - 1)
                for w, src in enumerate((AR[:, 0], Bd, Kd, XR[:, 8:12, :])):
                    if t:
                        pe.wait_ge(S["y_taken"], t)
                        pe.wait_ge(S["prev_tile"], t)
                    for g in range(NG):
                        ins = tr(PS[:, w, g * P:(g + 1) * P], src[:, g, tile], ident)
                    ins.then_inc(S["turned"], 1)
                for q in range(H):
                    g, lo = q % 4, 64 * (q // 4)
                    ins = mm(PS[:, 4 + q // 2, (q % 2) * 256:(q % 2) * 256 + 256], Bd[lo:lo + 64, g, tile],
                             AR[lo:lo + 64, :, g, tile], start=True, stop=True)
                    if q % 2:
                        ins.then_inc(S["gram_b"], 1)
                for q in range(H):
                    g, lo = q % 4, 64 * (q // 4)
                    if q % 4 == 0:
                        pe.wait_ge(S["turned_taken"], 4 * t + 1 + q // 4)
                    ins = mm(PS[:, q // 4, g * P:(g + 1) * P], AR[lo:lo + 64, 0, g, tile], Bd[lo:lo + 64, g, tile],
                             start=True, stop=True)
                    if q % 4 == 3:
                        ins.then_inc(S["gram_m"], 1)
                for q in range(H):
                    g, lo = q % 4, 64 * (q // 4)
                    if q % 2 == 0:
                        pe.wait_ge(S["gram_b_taken"], 4 * t + q // 2 + 1)
                    ins = mm(PS[:, 4 + q // 2, (q % 2) * 256:(q % 2) * 256 + 256], Kd[lo:lo + 64, g, tile],
                             AR[lo:lo + 64, :, g, tile], start=True, stop=True)
                    if q % 2:
                        ins.then_inc(S["gram_k"], 1)

                def turn_g(n, grp):
                    pe.wait_ge(S["turned_taken"], 4 * t + 4)
                    if n:
                        pe.wait_ge(S["x_taken"], 2 * (lev0 + (n - 1)) + grp + 1)
                    for i in range(4):
                        ins = tr(PS[:, 2 + grp, i * P:(i + 1) * P], MtRb[:, 4 * grp + i, 0, :], ident)
                    ins.then_inc(S["x_turned"], 1)

                pe.wait_ge(S["g_first"], t + 1)
                for grp in range(2):
                    turn_g(0, grp)
                pe.wait_ge(S["gram_k_taken"], 4 * t + 4)
                for l in range(nlev):
                    n = 2 * (lev0 + l)
                    for grp in range(2):
                        if l:
                            pe.wait_ge(S["g_added"], n + grp - 1)
                        for i in range(4):
                            q = 4 * grp + i
                            ins = mm(PS[:, 4 + grp, i * P:(i + 1) * P], Ms[:, q, :], MtRb[:, q, 0, :], start=True, stop=True)
                        ins.then_inc(S["r_ready"], 1)
                    for grp in range(2):
                        pe.wait_ge(S["r_taken"], n + grp + 1)
                        pe.wait_ge(S["x_taken"], n + grp + 1)
                        for i in range(4):
                            q = 4 * grp + i
                            ins = mm(PS[:, 6 + grp, i * P:(i + 1) * P], Xs[:, q, :], Rs[:, q, :], start=True, stop=True)
                        ins.then_inc(S["g_ready"], 1)
                    if l < nlev - 1:
                        for grp in range(2):
                            pe.wait_ge(S["g_added"], n + grp + 1)
                            turn_g(l + 1, grp)
                pe.wait_ge(S["g_added"], 2 * (lev0 + nlev))
                A_, B_, K_, V_ = range(4)
                for h in range(H):
                    q = 4 * (h % 2) + h // 2
                    hc = slice(h * HD, (h + 1) * HD)
                    ins = mm(PS[:, 0, hc], NtRk[:, q, 0, :], nat_[:, V_, hc], start=(h == 0), stop=(h == H - 1),
                             skip_group_check=True)
                ins.then_inc(S["nv_ready"], 1)
                for h in range(H):
                    g, hp = h // 2, h % 2
                    q, hc = 4 * hp + g, slice(h * HD, (h + 1) * HD)
                    ins = mm(PS[64 * hp:64 * hp + 64, 1, g * P:(g + 1) * P], nat_[:, A_, hc], MtRb[:, q, 0, :],
                             start=(g == 0), stop=(g == 3), skip_group_check=True)
                ins.then_inc(S["wt_ready"], 1)
                for h in range(H):
                    g, hp = h // 2, h % 2
                    q, hc = 4 * hp + g, slice(h * HD, (h + 1) * HD)
                    mm(PS[64 * hp:64 * hp + 64, 3, g * P:(g + 1) * P], nat_[:, V_, hc], NtRk[:, q, 1, :],
                       start=(g == 0), stop=False, skip_group_check=True)
                pe.wait_ge(S["nv_taken"], t + 1)
                for h in range(H):
                    q, hc = 4 * (h % 2) + h // 2, slice(h * HD, (h + 1) * HD)
                    mm(PS[:, 2, hc], MtRb[:, q, 0, :], NVs[:, hc], start=(h == 0), stop=False, skip_group_check=True)
                pe.wait_ge(S["wt_taken"], t + 1)
                for c in range(1 if t == 0 else 2):
                    r0, n = 64 * c, ch0 + c
                    rows = slice(r0, r0 + 64)
                    pe.wait_ge(S["st_done"], n + 1)
                    for g in range(NG):
                        ins = mm(PS[rows, 2, g * P:(g + 1) * P], Wt[:, g, rows], ST[:, g, :], start=False, stop=True,
                                 skip_group_check=True)
                    ins.then_inc(S["u_ready"], 1)
                    for g in range(NG):
                        mm(PS[:, 3, g * P + r0:g * P + r0 + 64], ST[:, g, :], AR[:, 1, g, c0 + r0:c0 + r0 + 64],
                           start=False, stop=False, skip_group_check=True)
                    for w in (K_, B_):
                        if w == B_:
                            pe.wait_ge(S["u_taken"], n + 1)
                        for h in range(H):
                            g, hp, hc = h // 2, h % 2, slice(h * HD, (h + 1) * HD)
                            src = nat_[rows, V_, hc] if w == K_ else Us[rows, hc]
                            ins = mm(PS[64 * hp:64 * hp + 64, 4, g * HD:(g + 1) * HD], nat_[rows, w, hc], src,
                                     start=(w == K_ and g == 0), stop=(w == B_), skip_group_check=True)
                    ins.then_inc(S["st_ready"], 1)
                if t == 0:
                    pe.wait_ge(S["s0_in0"], 128)
                    for b in range(DB):
                        if b == DB // 2:
                            pe.wait_ge(S["s0_in1"], 128)
                        if b >= 2:
                            pe.wait_ge(S["s0_taken"], b - 1)
                        for g in range(NG):
                            ins = tr(PS[:, 6 + b % 2, g * P:(g + 1) * P], S0n[:, b % (DB // 2), g, :], ident)
                        ins.then_inc(S["s0_turned"], 1)
                    pe.wait_ge(S["s0_taken"], DB)
                    for b in range(DB):
                        tok = slice(64 + DS * b, 64 + DS * (b + 1))
                        for g in range(NG):
                            mm(PS[:, 5, g * NS + DS * b:g * NS + DS * (b + 1)], S0T[:, b, g, :], Wt[:, g, tok],
                               start=(b == 0 and g == 0), stop=True, skip_group_check=True)
                            ins = mm(PS[:, 3, g * P + tok.start:g * P + tok.stop], S0T[:, b, g, :], AR[:, 1, g, tok],
                                     start=False, stop=False, skip_group_check=True)
                    ins.then_inc(S["ut_ready"], 1)
                    pe.wait_ge(S["ut_taken"], 1)
                    for g in range(NG):
                        ins = mm(PS[64:P, 2, g * P:(g + 1) * P], UTs[:, g, :], ident, start=False, stop=True,
                                 skip_group_check=True)
                    ins.then_inc(S["us_ready"], 1)
                    pe.wait_ge(S["us_taken"], 1)
                else:
                    pe.wait_ge(S["u_taken"], ch0 + 2)
                for h in range(H):
                    g, hp = h // 2, h % 2
                    q, hc = 4 * hp + g, slice(h * HD, (h + 1) * HD)
                    ins = mm(PS[64 * hp:64 * hp + 64, 3, g * P:(g + 1) * P], Us[:, hc], MtRb[:, q, 1, :],
                             start=False, stop=(g == 3), skip_group_check=True)
                ins.then_inc(S["y_ready"], 1)
                if t == 0:
                    for g in range(NG):
                        for hp in range(2):
                            h = 2 * g + hp
                            hc = slice(h * HD, (h + 1) * HD)
                            pe.wait_ge(S["um_ready"], h + 1)
                            o = PS[64 * hp:64 * hp + 64, 6 + g % 2, :]
                            if g >= 2 and hp == 0:
                                pe.wait_ge(S["sn_taken"], g - 1)
                            mm(o, nat_[64:P, K_, hc], Um[64:P, 1].rearrange("p b i -> p (b i)"), start=True, stop=False)
                            ins = mm(o, nat_[64:P, B_, hc], Um[64:P, 0].rearrange("p b i -> p (b i)"), start=False, stop=True)
                            ins.then_inc(S["sn_ready"], 1)
                    for g in range(NG):
                        pe.wait_ge(S["sn_taken"], g + 1)
                        if g:
                            pe.wait_ge(S["so_taken"], g)
                        for b in range(DB):
                            ins = tr(PS[0:64, b // 4, (b % 4) * P:(b % 4 + 1) * P], Sn[:, g, b * HD:(b + 1) * HD], ident)
                        ins.then_inc(S["so_turned"], 1)
                    pe.wait_ge(S["so_taken"], NG)
            pe.wait_ge(S["st_done"], 10)
            pe.wait_ge(S["y_taken"], NTILE)
            for g in range(NG):
                ins = tr(PS[:, 0, g * P:(g + 1) * P], ST[:, g, :], ident)
            ins.then_inc(S["fs_turned"], 1)
            pe.wait_ge(S["fs_taken"], 1)
            head_sums(YT, 3)
            head_sums(T2, 4)
            pe.wait_ge(S["hs_taken"], 16)

            pe.wait_ge(S["rwkv_done"], 1)
            pe.wait_ge(S["ln_in"], 32)
            for n in range(4):
                t, h0 = n // 2, 4 * (n % 2)
                lv = Ln[:, t, :].rearrange("p (k h) -> p h k", h=H)
                for h in range(4):
                    ins = tr(PS[:, n, h * P:(h + 1) * P], lv[:, h0 + h, :], ident)
                ins.then_inc(S["lt_turned"], 1)
            pe.wait_ge(S["tu_ready"], 1)
            for n in range(4):
                t, h0 = n // 2, 4 * (n % 2)
                pe.wait_ge(S["lt_taken"], n + 1)
                mm(PS[:, 4 + n, :], later_key, LTk[:, t, h0:h0 + 4, :].rearrange("p h n -> p (h n)"), start=True, stop=False)
                mm(PS[:, 4 + n, :], ones, TU[:, t, h0:h0 + 4, :].rearrange("p h n -> p (h n)"), start=False, stop=True)\
                    .then_inc(S["r_sums"], 1)
            pe.wait_ge(S["rl_taken"], 4)

            def turn_keys(b, p):
                if p % LOT == 0:
                    pe.wait_ge(k_in[p % NRING // LOT], LOT * (32 * b + 16 * (p // NRING + 1)))
                if p >= 2 or not (isinstance(b, int) and b == 0):
                    pe.wait_ge(S["kt_taken"], b * NPG + (p - 1))
                for g in range(NG):
                    ins = tr(PS[:, p % 2, g * P:(g + 1) * P], Kr[:, p % NRING, g * P:(g + 1) * P], ident)
                ins.then_inc(S["k_free"], 1)

            def page_scores(b, p):
                j = p // 8
                pe.wait_ge(S["kt_taken"], b * NPG + (p + 1))
                if p % 8 == 0 and (j >= 2 or not (isinstance(b, int) and b == 0)):
                    pe.wait_ge(S["sc_taken"], b * 4 + (j - 1))
                for g in range(NG):
                    c = (p % 8) * 64 + g * 16
                    ins = mm(PS[:, 2 + j % 2, c:c + 16], KTs[:, p % 2, g, :], QB[:, bass.ds(b, 1), g, :].rearrange("p o c -> p (o c)"),
                             start=(p % 8 == 0 and g == 0), stop=True, skip_group_check=True)
                ins.then_inc(S["sc_page"], 1)

            def new_scores(b):
                for g in range(NG):
                    ins = mm(PS[:, 6, g * 16:(g + 1) * 16], kTS[:, g, :], QB[:, bass.ds(b, 1), g, :].rearrange("p o c -> p (o c)"),
                             start=(g == 0), stop=True, skip_group_check=True)
                ins.then_inc(S["new_ready"], 1)

            def page_values(b, p):
                if p < NPG and p % LOT == 0:
                    pe.wait_ge(v_in[p % NRING // LOT], LOT * (32 * b + 16 * (p // NRING + 1)))
                for g in range(NG):
                    w = vnat[:, 0, g * P:(g + 1) * P] if p == NPG else Vr[:, p % NRING, g * P:(g + 1) * P]
                    ins = mm(PS[:, 4, g * 16:(g + 1) * 16], w, Pb[:, p, g * 16:(g + 1) * 16],
                             start=(p == NPG and g == 0), stop=(p == NPG - 1), skip_group_check=True)
                if p < NPG:
                    ins.then_inc(S["v_free"], 1)

            def row_max(b):
                pe.wait_ge(S["mx_in"], b + 1)
                tr(PS[:, 7, 0:P], mx, ident).then_inc(S["mx_turned"], 1)
                pe.wait_ge(S["dg_ready"], b + 1)
                mm(PS[:, 7, P:P + 64], ones[0:64, :], dg[0:64, :], start=True, stop=True).then_inc(S["mx_spread"], 1)

            def row_sum(b):
                pe.wait_ge(S["sm_ready"], b + 1)
                mm(PS[:, 5, 0:64], ones, sm, start=True, stop=True).then_inc(S["sum_ready"], 1)

            def pass_pages(b, prev):
                for p in range(NPG):
                    turn_keys(b, p)
                    if p == 0:
                        new_scores(b)
                    if p:
                        page_scores(b, p - 1)
                    if prev and p == 8:
                        row_sum(b - 1)
                        pe.wait_ge(S["exp_out"], (b - 1) * 2 + 2)
                        page_values(b - 1, NPG)
                    if prev and p >= 8:
                        page_values(b - 1, p - 8)
                page_scores(b, NPG - 1)
                if prev:
                    for p in range(NPG - 8, NPG):
                        page_values(b - 1, p)
                row_max(b)

            pass_pages(0, False)
            with pe.Fori(1, DB) as b:
                pass_pages(b, True)
            row_sum(DB - 1)
            pe.wait_ge(S["exp_out"], 2 * DB)
            page_values(DB - 1, NPG)
            for p in range(NPG):
                page_values(DB - 1, p)

            def rows_of(i):
                return (slice(64, P), slice(SEQ, OUTC)) if i == 0 else (slice(0, P), slice((i - 1) * P, i * P))

            pe.wait_ge(S["attn_done"], 1)
            pe.wait_ge(S["wo_in"], 16)
            order = [1, 2, 3, 4, 0]
            def project(n):
                rows, cols = rows_of(order[n])
                if n >= 2:
                    pe.wait_ge(S["h_ready"], n - 1)
                for half in range(2):
                    for k in range(KT):
                        ins = mm(PS[rows, 2 * (n % 2) + half, :], mixT[:, k, cols], wo[:, k, half * NB:(half + 1) * NB],
                                 start=(k == 0), stop=(k == KT - 1))
                ins.then_inc(S["mixed_out"], 1)

            def turn_h(n):
                rows, cols = rows_of(order[n])
                w = cols.stop - cols.start
                pe.wait_ge(S["xs_ready"], NTILE + n + 1)
                if n >= 2:
                    pe.wait_ge(S["xnT_ready"], NTILE + n - 1)
                for f in range(KT):
                    ins = tr(PS[:, 4 + 2 * (n % 2) + f // 4, (f % 4) * w:(f % 4 + 1) * w], xs2[rows, n % 2, f * P:(f + 1) * P],
                             ident[rows, rows])
                ins.then_inc(S["xT_turned"], 1)

            for n in range(NTILE + 2):
                if n < NTILE:
                    project(n)
                if n >= 2:
                    turn_h(n - 2)
            pe.wait_ge(S["xnT_ready"], 2 * NTILE)
            HO = OUTC // 2
            for f in range(NF):
                r = f // 2
                if f % 2 == 0:
                    pe.wait_ge(f_in[r % FR], 32 * (r // FR + 1))
                if f >= 2:
                    pe.wait_ge(S["act_ready"], f - 1)
                for w in range(2):
                    for half in range(2):
                        for k in range(KT):
                            c = w * 2048 + k * 256 + (f % 2) * P
                            ins = mm(PS[:, 4 * (f % 2) + 2 * w + half, 0:HO], fring[:, r % FR, c:c + P],
                                     hT[:, k, half * HO:(half + 1) * HO], start=(k == 0), stop=(k == KT - 1))
                ins.then_inc(S["gu_ready"], 1)
            pe.wait_ge(S["act_ready"], NF)
            for half in range(2):
                for c in range(3):
                    r = 11 + 3 * half + c
                    pe.wait_ge(f_in[r % FR], 32 * (r // FR + 1))
                    for k in range(8 * c, min(8 * c + 8, NF)):
                        for n, i in enumerate(order):
                            rows, cols = rows_of(i)
                            if half and k == 0 and n >= 3:
                                pe.wait_ge(S["down_taken"], n - 2)
                            ins = mm(PS[rows, (5 * half + n) % 8, :], actT[:, k, cols],
                                     fring[:, r % FR, (k - 8 * c) * NB:(k - 8 * c + 1) * NB], start=(k == 0), stop=(k == NF - 1))
                            if k == NF - 1 and n < NTILE - 1:
                                ins.then_inc(S["down_tile"], 1)
                    ins.then_inc(S["down_used"], 1)

        @block.scalar
        def _(act):
            ch = Chain(act, S["act_c"])
            av = nc.scalar.activation
            act.wait_ge(S["par_turned"], 1)
            av(par[:, 0:NPAR], PS[:, 7, 0:NPAR], ACT.Copy).then_inc(S["par_ready"], 1)
            for i in range(NTILE):
                act.wait_ge(x_in[i], 48 if i == 0 else 16)
                if i == 0:
                    act.wait_ge(S["consts"], 1)
                ch(av(xsq, x[:, i, :], ACT.Square, accum_out=ss[:, i:i + 1]))
                ch.wait()
                nc.scalar.activation(rstd[:, i:i + 1], ss[:, i:i + 1], ACT.Copy).then_inc(S["square_done"], 1)
                act.wait_ge(S["var_done"], i + 1)
                av(ss[:, i:i + 1], rstd[:, i:i + 1], ACT.Sqrt).then_inc(S["std_done"], 1)
            act.wait_ge(S["shn_turned"], 1)
            av(shn[0:9, :].rearrange("p (a b) -> p a b", a=2), PS[0:9, 4:6, :], ACT.Copy).then_inc(S["shn_ready"], 1)
            for n, (c, c0, width, dest) in enumerate(ITEMS):
                act.wait_ge(S["proj_ready"], n + 1)
                src = PS[0:width, 2 * (n % 3):2 * (n % 3) + 2, 0:HALF]
                kind, g = dest
                if kind == "rw":
                    if g >= 2:
                        act.wait_ge(S["mixed_done"], g - 1)
                    dst, scale = raw[:, g % 2, :], 1.0
                elif kind == "f":
                    dst, scale = fT[0:H], 1.0
                else:
                    dst, scale = (qT if kind == "q" else kT)[:, g, :], (HD ** -0.5 if kind == "q" else 1.0)
                av(dst.rearrange("p (a b) -> p a b", a=2), src, ACT.Copy, scale=scale).then_inc(S["proj_taken"], 1)
                if kind == "f":
                    act.wait_ge(S["f_in"], 16)
                    act.wait_ge(S["proj_taken"], n + 1)
                    ch(av(cT[0:H], fT[0:H], ACT.Abs, bias=bf_col[0:H]))
                    ch.wait()
                    ch(av(cT[0:H], cT[0:H], ACT.Exp, scale=-1.0))
                    ch.wait()
                    av(f2[0:H], cT[0:H], ACT.Ln, bias=1.0).then_inc(S["logf_a"], 1)
            for h in range(H):
                act.wait_ge(S["ncb_ready"], h + 1)
                av(NCB[:, h, :].rearrange("p (a b) -> p a b", a=2), PS[:, 2 * (h % 3):2 * (h % 3) + 2, 0:NPT // 2],
                   ACT.Copy, scale=-1.0).then_inc(S["ncb_taken"], 1)

            def take_pt(n):
                i = n // 2 % 4
                act.wait_ge(S["pt_ready"], n + 1)
                if n >= 2:
                    act.wait_ge(S["pv_ready"], n - 1)
                av(PT[:, n % 2, 0:i + 1, :], PS[:, 4, 0:(i + 1) * P].rearrange("p (a b) -> p a b", b=P), ACT.Copy)
                av(PT[0:NMETA, n % 2, 4, :], PS[0:NMETA, 5, 0:P], ACT.Copy).then_inc(S["pt_taken"], 1)

            def take_o(it):
                act.wait_ge(S["pv_ready"], 2 * it + 2)
                g, i = it // 4, it % 4
                av(mixT[:, g, i * P:(i + 1) * P], PS[:, 6 + it % 2, 0:P], ACT.Copy).then_inc(S["o_taken"], 1)

            for n in range(32):
                i = n // 2 % 4
                act.wait_ge(S["mx_ready"], n + 1)
                sv = Sp[:, n % 2, 0:NMETA + P * (i + 1)]
                av(sv, sv, ACT.Exp, bias=nmp[:, n % 2:n % 2 + 1], accum_out=smp[:, n % 2:n % 2 + 1]).then_inc(S["exp_done"], 1)
                if n >= 1:
                    take_pt(n - 1)
                if n >= 2 and n % 2 == 0:
                    take_o((n - 2) // 2)
            take_pt(31)
            take_o(15)

            ch.wait()
            act.wait_ge(S["mixed_done"], 14)
            av(XR[0:64, 12, :], XR[0:64, 12, :], ACT.Tanh).then_inc(S["lr_act"], 1)
            av(XR[:, 13, :], XR[:, 13, :], ACT.Sigmoid).then_inc(S["lr_act"], 1)
            act.wait_ge(S["pv_ready"], 32)
            for j in range(12):
                g = j % 4
                act.wait_ge(S["lr_ready"], j + 1)
                src = PS[:, 2 * (j % 3):2 * (j % 3) + 2, 0:TL // 2]
                dst = (AR[:, 0, g] if j < 4 else Bd[:, g] if j < 8 else gate[:, g]).rearrange("p (a b) -> p a b", a=2)
                if j < 8:
                    av(dst, src, ACT.Sigmoid, bias=pc("w0" if j < 4 else "a0", g)).then_inc(S["lr_taken"], 1)
                else:
                    av(dst, src, ACT.Copy).then_inc(S["lr_taken"], 1)
            act.wait_ge(S["L_ready"], 1)
            av(AR[:, 1], Kd, ACT.Exp).then_inc(S["decays"], 1)
            av(AR[:, 0], AR[:, 0], ACT.Exp).then_inc(S["decays"], 1)
            act.wait_ge(S["decays"], 1)
            av(Kd, Kd, ACT.Exp, scale=-1.0).then_inc(S["decays"], 1)
            act.wait_ge(S["root_in"], 1)
            av(T2, T2, ACT.Sqrt).then_inc(S["root_done"], 1)

            act.wait_ge(S["pre_done"], 1)
            for t in range(NTILE):
                nlev = 3 if t == 0 else 5
                lev0 = 0 if t == 0 else 3 + 5 * (t - 1)
                if t:
                    act.wait_ge(S["y_ready"], t)
                    act.wait_ge(S["st_ready"], 1 + 2 * (t - 1))
                    if t == 1:
                        act.wait_ge(S["sn_ready"], H)
                for w in range(4):
                    act.wait_ge(S["turned"], 4 * t + w + 1)
                    av(nat_[:, w, :], PS[:, w, :], ACT.Copy).then_inc(S["turned_taken"], 1)
                for l in range(nlev):
                    for grp in range(2):
                        n = 2 * (lev0 + l) + grp
                        act.wait_ge(S["x_turned"], n + 1)
                        if l:
                            act.wait_ge(S["g_ready"], n - 1)
                        av(Xs[:, 4 * grp:4 * grp + 4, :], PS[:, 2 + grp, :].rearrange("p (a b) -> p a b", a=4),
                           ACT.Copy).then_inc(S["x_taken"], 1)
                act.wait_ge(S["nv_ready"], t + 1)
                av(NVs, PS[:, 0, :], ACT.Copy).then_inc(S["nv_taken"], 1)
                act.wait_ge(S["wt_ready"], t + 1)
                av(Wt, PS[:, 1, :].rearrange("p (a b) -> p a b", a=NG), ACT.Copy).then_inc(S["wt_taken"], 1)
                if t == 0:
                    for b in range(DB):
                        act.wait_ge(S["s0_turned"], b + 1)
                        av(S0T[:, b], PS[:, 6 + b % 2, :].rearrange("p (a b) -> p a b", a=NG), ACT.Copy).then_inc(S["s0_taken"], 1)
                    act.wait_ge(S["ut_ready"], 1)
                    av(UTs, PS[:, 5, 0:NG * NS].rearrange("p (a b) -> p a b", a=NG), ACT.Copy).then_inc(S["ut_taken"], 1)
                act.wait_ge(S["y_ready"], t + 1)
                av(YT[:, :, t * P:(t + 1) * P], PS[:, 3, :].rearrange("p (a b) -> p a b", a=NG), ACT.Copy).then_inc(S["y_taken"], 1)
                if t == 0:
                    for g in range(NG):
                        act.wait_ge(S["so_turned"], g + 1)
                        if g >= 2:
                            act.wait_ge(S[f"so_out{g % 2}"], 32)
                        av(SOo[0:64, g % 2], PS[0:64, 0:2, :].rearrange("p a (b c) -> p (a b) c", b=4), ACT.Copy)\
                            .then_inc(S["so_taken"], 1)
            act.wait_ge(S["fs_turned"], 1)
            av(Xs[:, 0:NG, :], PS[:, 0, :].rearrange("p (a b) -> p a b", a=NG), ACT.Copy).then_inc(S["fs_taken"], 1)
            act.wait_ge(S["yc_ready"], 1)
            act.wait_ge(S["fs_out"], 32)
            av(T2, YT, ACT.Square).then_inc(S["hs_in"], 1)
            act.wait_ge(S["root_in"], 2)
            av(T2, T2, ACT.Sqrt).then_inc(S["root_done"], 1)

            for n in range(4):
                t, h0 = n // 2, 4 * (n % 2)
                act.wait_ge(S["lt_turned"], n + 1)
                av(LTk[:, t, h0:h0 + 4, :], PS[:, n, :].rearrange("p (h n) -> p h n", h=4), ACT.Copy).then_inc(S["lt_taken"], 1)
            for n in range(4):
                t, h0 = n // 2, 4 * (n % 2)
                act.wait_ge(S["r_sums"], n + 1)
                for b in range(4):
                    ins = av(Rl[:, 4 * t + b, h0:h0 + 4, :],
                             PS[:, 4 + n, :].rearrange("p (h b c) -> p h b c", h=4, b=4)[:, :, b, :], ACT.Copy)
                ins.then_inc(S["rl_taken"], 1)

            def take_keys(b, p):
                act.wait_ge(S["k_free"], b * NPG + (NRING + p + 1))
                if p >= 2 or not (isinstance(b, int) and b == 0):
                    act.wait_ge(S["sc_page"], b * NPG + (p - 1))
                av(KTs[:, p % 2], PS[:, p % 2, :].rearrange("p (g n) -> p g n", g=NG), ACT.Copy).then_inc(S["kt_taken"], 1)

            def exps(b):
                for part in range(2):
                    act.wait_ge(S["p_in"], b * 2 + (part + 1))
                    w = Pb[:, 16:NPG + 1, :] if part else Pb[:, 0:16, :]
                    av(w, w, ACT.Exp).then_inc(S["exp_out"], 1)

            for p in range(NPG):
                take_keys(0, p)
            with act.Fori(1, DB) as b:
                for p in range(NPG):
                    take_keys(b, p)
                    if p == 3:
                        exps(b - 1)
            exps(DB - 1)

            def mean_of_squares(n, i, turn):
                rows = slice(64, P) if i == 0 else slice(0, P)
                act.wait_ge(S["h_ready"], turn * NTILE + n + 1)
                act.wait_ge(S["square_done"], (turn + 1) * NTILE + n)
                ch(av(xsq2[rows], x[rows, i, :], ACT.Square, accum_out=ss[rows, i:i + 1]))
                ch.wait()
                av(rstd[rows, i:i + 1], ss[rows, i:i + 1], ACT.Copy).then_inc(S["square_done"], 1)
                act.wait_ge(S["var_done"], (turn + 1) * NTILE + n + 1)
                av(ss[rows, i:i + 1], rstd[rows, i:i + 1], ACT.Sqrt).then_inc(S["std_done"], 1)

            for n, i in enumerate([1, 2, 3, 4, 0]):
                mean_of_squares(n, i, 0)
            HO = OUTC // 2
            for f in range(NF):
                act.wait_ge(S["gu_ready"], f + 1)
                if f >= 2:
                    act.wait_ge(S["act_ready"], f - 1)
                av(sgate[:, f % 2, :].rearrange("p (a b) -> p a b", a=2), PS[:, 4 * (f % 2):4 * (f % 2) + 2, 0:HO], ACT.Silu)\
                    .then_inc(S["silu_done"], 1)
            for n, i in enumerate([1, 2, 3, 4, 0]):
                mean_of_squares(n, i, 1)

        @block.vector
        def _(dve):
            ch = Chain(dve, S["dve_c"])
            v = nc.vector
            tt, ts, stt = v.tensor_tensor, v.tensor_scalar, v.scalar_tensor_tensor
            dve.wait_ge(S["consts"], 1)

            def mean_square(i):
                dve.wait_ge(S["square_done"], i + 1)
                ts(rstd[:, i:i + 1], rstd[:, i:i + 1], 1.0 / D, RMS_EPS, ALU.mult, ALU.add).then_inc(S["var_done"], 1)

            for i in range(NTILE):
                mean_square(i)
                dve.wait_ge(S["std_done"], i + 1)
                ch(v.reciprocal(rstd[:, i:i + 1], ss[:, i:i + 1]))
                ch.wait()
                if i == 0:
                    ch(v.memset(rstd[32:32 + DB, 0:1], 1.0))
                    ch.wait()
                if i >= 2:
                    dve.wait_ge(S["xT_turned"], i - 1)
                ts(xs[:, i % 2, :], x[:, i, :], rstd[:, i:i + 1], None, ALU.mult).then_inc(S["xs_ready"], 1)
                if i == 0:
                    dve.wait_ge(S["par_ready"], 1)
                dve.wait_ge(S["xT_turned"], i + 1)
                for hf in range(2):
                    gain = par[:, pcol["ln1_g"] + 4 * hf:pcol["ln1_g"] + 4 * hf + 4].unsqueeze(2)
                    src = PS[:, 2 * (i % 2) + hf, :].rearrange("p (f c) -> p f c", c=P)
                    dst = xnT[:, 4 * hf:4 * hf + 4, :]
                    if i:
                        ins = tt(dst[:, :, 17 + P * (i - 1):17 + P * i], src, gain.to_broadcast([P, 4, P]), ALU.mult)
                    else:
                        tt(dst[:, :, 1:1 + NMETA], src[:, :, 0:NMETA], gain.to_broadcast([P, 4, NMETA]), ALU.mult)
                        for k in range(4):
                            ts(samp(dst[:, k, :], 1), src[:, k, 64:P].rearrange("p (b t) -> p b t", t=DS),
                               pc("ln1_g", 4 * hf + k), None, ALU.mult)
                        ins = v.tensor_copy(dst[:, :, RS0:RS0 + 9 * DB:9], src[:, :, 32:32 + DB])
                if i == 0:
                    ch(ins)
                    ch.wait()
                    ins = v.tensor_copy(xnS.rearrange("p k (b t) -> p k b t", t=DS), samps(xnT))
                ins.then_inc(S["xnT_ready"], 1)

            def take_nat(j):
                dve.wait_ge(S["nat_ready"], j + 1)
                src = PS[:, 6 + j % 2, :]
                if j < NTILE:
                    if j == 0:
                        v.tensor_copy(vnat[0:NMETA, 0, :], src[0:NMETA])
                        ins = v.tensor_copy(vnat[64:P, 0, :], src[64:P])
                    else:
                        ins = v.tensor_copy(vnat[:, j, :], src)
                elif j < NTILE + 6:
                    n = (NMETA, P, P, P, P, NS)[j - NTILE]
                    ins = v.tensor_copy(kn[64:P, 0, :] if n == NS else kn[0:n, j - NTILE, :], src[0:n])
                else:
                    v.tensor_copy(cnat, src[:, NTILE * H:(NTILE + 1) * H])
                    ins = v.tensor_copy(lognat, src[:, 0:NTILE * H].rearrange("p (i h) -> p i h", h=H))
                ins.then_inc(S["nat_taken"], 1)

            dve.wait_ge(S["proj_taken"], 2 * NG)
            v.tensor_copy(kTS[:, :, 64:P].rearrange("p g (b t) -> p g b t", t=DS), samps(kT)).then_inc(S["kts_ready"], 1)
            for j in range(11):
                take_nat(j)
            dve.wait_ge(S["logf_a"], 1)
            dve.wait_ge(S["f_in"], 16)
            ch(ts(fT[0:H], fT[0:H], bf_col[0:H], 0.0, ALU.add, ALU.min))
            ch.wait()
            ch(tt(fT[0:H], fT[0:H], f2[0:H], ALU.subtract))
            ch.wait()
            ch(v.tensor_tensor_scan(cT[0:H], forget_mask[0:H], fT[0:H], 0.0, ALU.mult, ALU.add))
            ch.wait()
            v.tensor_copy(LT[0:H, 0:NMETA], fT[0:H, 1:1 + NMETA])
            v.tensor_copy(LT[0:H, 64:P].rearrange("p (b t) -> p b t", t=DS), samp(fT[0:H], 1))
            v.tensor_copy(LT[0:H, P:TL], fT[0:H, 17:17 + SEQ])
            v.memset(f2[0:H, 0:64], 0.0)
            v.tensor_copy(f2[0:H, 64:P].rearrange("p (b t) -> p b t", t=DS), samp(cT[0:H], 1)).then_inc(S["log_ready"], 1)

            for n in range(14):
                dve.wait_ge(S["proj_taken"], NRW0 + n + 1)
                r = raw[:, n % 2, :]
                if n:
                    dve.wait_ge(S["mixed_done"], n)
                ch(tt(diff[:, 0:RAW - 1], r[:, 0:RAW - 1], r[:, 1:RAW], ALU.subtract))
                ch.wait()
                mu = pc("mu_shift", n)
                stt(XR[:, n, 0:NMETA], diff[:, 0:NMETA], mu, r[:, 1:1 + NMETA], ALU.mult, ALU.add)
                stt(XR[:, n, 64:P].rearrange("p (b t) -> p b t", t=DS), samp(diff, 0), mu, samp(r, 1), ALU.mult, ALU.add)
                stt(XR[:, n, P:TL], diff[:, 16:16 + SEQ], mu, r[:, 17:17 + SEQ], ALU.mult, ALU.add).then_inc(S["mixed_done"], 1)
            take_nat(11)
            dve.wait_ge(S["nat_taken"], 12)
            ch(tt(RN[64:P], RN[64:P], cnat[64:P].unsqueeze(1).unsqueeze(3).to_broadcast([64, DB, H, DS]), ALU.subtract))
            for hp in range(2):
                for g in range(NG):
                    ins = v.tensor_copy(QB[64 * hp:64 * hp + 64, :, g, 8 * hp:8 * hp + 8], samp(qT[64 * hp:64 * hp + 64, g, :], 1))
            ins.then_inc(S["qb_ready"], 1)
            dve.wait_ge(S["proj_ready"], len(ITEMS))
            v.memset(PT[:, :, 4, :], 0.0).then_inc(S["pt_zero"], 1)

            dve.wait_ge(S["ncb_taken"], H)
            for n in range(33):
                if n < 32:
                    g, i, hp = n // 8, n // 2 % 4, n % 2
                    nk = NMETA + P * (i + 1)
                    sv = Sp[:, n % 2, 0:nk]
                    dve.wait_ge(S["s_ready"], n + 1)
                    if n >= 2:
                        dve.wait_ge(S["pt_ready"], n - 1)
                    tt(sv.rearrange("p (a b) -> p a b", a=2), PS[:, 2 * hp:2 * hp + 2, 0:nk // 2],
                       NCB[:, 2 * g + hp, 0:nk].rearrange("p (a b) -> p a b", a=2), ALU.add).then_inc(S["s_added"], 1)
                    dve.wait_ge(S["s_added"], n + 1)
                    ch(tt(sv[:, nk - P:nk], sv[:, nk - P:nk], causal, ALU.add))
                    ch.wait()
                    ch(v.tensor_reduce(mxp[:, n % 2:n % 2 + 1], sv, AX.X, ALU.max))
                    ch.wait()
                    ts(nmp[:, n % 2:n % 2 + 1], mxp[:, n % 2:n % 2 + 1], -1.0, None, ALU.mult).then_inc(S["mx_ready"], 1)
                if n >= 1:
                    m = n - 1
                    if m >= 2:
                        dve.wait_ge(S["p_ready"], m)
                    dve.wait_ge(S["exp_done"], m + 1)
                    nk = NMETA + P * (m // 2 % 4 + 1)
                    ch(v.reciprocal(rcp[:, m % 2:m % 2 + 1], smp[:, m % 2:m % 2 + 1]))
                    ch.wait()
                    sv = Sp[:, m % 2, 0:nk]
                    ts(sv, sv, rcp[:, m % 2:m % 2 + 1], None, ALU.mult).then_inc(S["p_ready"], 1)

            HT = TL // 2

            def two(w):
                return w.rearrange("p (a b) -> p a b", a=2)

            def hs(n):
                return PS[:, 2 * (n % 3):2 * (n % 3) + 2, 0:HT]

            dve.wait_ge(S["lr_taken"], 8)
            ch(ts(AR[:, 0], AR[:, 0], -E_HALF, None, ALU.mult))
            ch.wait()
            for g in range(NG):
                ch(v.tensor_tensor_scan(Kd[:, g], chunk_mask, AR[:, 0, g], 0.0, ALU.mult, ALU.add))
            ch.wait()
            tt(AR[:, 0], Kd, AR[:, 0], ALU.subtract).then_inc(S["L_ready"], 1)
            dve.wait_ge(S["out_done"], 16 * N_FIRST_OUT)
            for g in range(NG):
                ch(ts(kk[:, g], XR[:, 4 + g], pc("k_k", g), None, ALU.mult))
            ch.wait()
            tt(T2, kk, kk, ALU.mult).then_inc(S["hs_in"], 1)
            dve.wait_ge(S["hs_in"], 1)
            for g in range(NG):
                dve.wait_ge(S["hs_ready"], g + 1)
                ts(two(T2[:, g]), hs(g), 1e-24, None, ALU.max).then_inc(S["hs_taken"], 1)
            dve.wait_ge(S["hs_taken"], 4)
            v.memset(small[:, 0:1], 0.0).then_inc(S["root_in"], 1)
            dve.wait_ge(S["root_done"], 1)
            ch(v.reciprocal(T2, T2))
            ch.wait()
            ch(tt(kk, kk, T2, ALU.mult))
            ch.wait()
            for g in range(NG):
                ch(ts(T2[:, g], Bd[:, g], -1.0, pc("k_a", g), ALU.add, ALU.mult))
            ch.wait()
            ch(stt(XR[:, 4:8], T2, 1.0, XR[:, 4:8], ALU.add, ALU.mult))
            ch.wait()
            for g in range(NG):
                ins = stt(T2[:, g], XR[:, g], pc("r_k", g), XR[:, 4 + g], ALU.mult, ALU.mult)
            ins.then_inc(S["hs_in"], 1)
            dve.wait_ge(S["decays"], 3)
            ch(tt(Bd, Bd, kk, ALU.mult))
            ch(stt(AR[:, 0], kk, -1.0, AR[:, 0], ALU.mult, ALU.mult))
            ch(v.tensor_copy(Dc[:, :, 0:1], AR[:, 1, :, NMETA - 1:NMETA]))
            ch(v.tensor_copy(Dc[:, :, 1:1 + DB], AR[:, 1, :, 64 + DS - 1:P:DS]))
            ch(v.tensor_copy(Dc[:, :, 1 + DB:], AR[:, 1, :, P + 63:TL:64]))
            ch.wait()
            ch(tt(Bd, Bd, Kd, ALU.mult))
            ch(tt(AR[:, 1], XR[:, 0:4], AR[:, 1], ALU.mult))
            ch.wait()
            ch(tt(Kd, XR[:, 4:8], Kd, ALU.mult))
            for g in range(NG):
                dve.wait_ge(S["hs_ready"], NG + g + 1)
                tt(two(kk[:, g]), hs(NG + g), two(XR[:, 8 + g]), ALU.mult).then_inc(S["hs_taken"], 1)
            ch.wait()
            dve.wait_ge(S["hs_taken"], 2 * NG)
            ch(v.memset(S0n, 0.0))
            ch(v.memset(ST, 0.0))
            ch.wait()
            v.memset(Us, 0.0).then_inc(S["pre_done"], 1)
            dve.wait_ge(S["pre_done"], 1)
            v.memset(small[:, 1:2], 0.0).then_inc(S["st_done"], 1)

            for t in range(NTILE):
                nlev = 3 if t == 0 else 5
                lev0 = 0 if t == 0 else 3 + 5 * (t - 1)
                ch0 = 0 if t == 0 else 1 + 2 * (t - 1)
                kind = 0 if t == 0 else 1

                def masked(dst, src, mask, k):
                    return tt(dst, src, mask.unsqueeze(1).to_broadcast([P, k, P]), ALU.mult)

                if t == 0:
                    dve.wait_ge(S["lr_ready"], 12)
                else:
                    dve.wait_ge(S["y_ready"], t)
                if t == 1:
                    dve.wait_ge(S["so_out0"], 64)
                    dve.wait_ge(S["so_out1"], 64)
                    dve.wait_ge(S["um_used"], H)
                for j in range(4):
                    dve.wait_ge(S["gram_b"], 4 * t + j + 1)
                    src = PS[:, 4 + j, :].rearrange("p (q w c) -> p q w c", q=2, w=2)
                    masked(MtRb[:, 2 * j:2 * j + 2, 0, :], src[:, :, 0, :], level[:, 0, :], 2)
                    masked(MtRb[:, 2 * j:2 * j + 2, 1, :], src[:, :, 1, :], up_incl[:, kind, :], 2).then_inc(S["gram_b_taken"], 1)
                dve.wait_ge(S["gram_b_taken"], 4 * t + 4)
                tt(MtRb[:, :, 0, :], MtRb[:, :, 0, :], ident.unsqueeze(1).to_broadcast([P, H, P]), ALU.add).then_inc(S["g_first"], 1)
                for j in range(2):
                    dve.wait_ge(S["gram_m"], 2 * t + j + 1)
                    ch(masked(Ms[:, 4 * j:4 * j + 4, :], PS[:, j, :].rearrange("p (q c) -> p q c", q=4), low_strict[:, kind, :], 4))
                for j in range(4):
                    dve.wait_ge(S["gram_k"], 4 * t + j + 1)
                    src = PS[:, 4 + j, :].rearrange("p (q w c) -> p q w c", q=2, w=2)
                    masked(NtRk[:, 2 * j:2 * j + 2, 0, :], src[:, :, 0, :], up_strict[:, kind, :], 2)
                    masked(NtRk[:, 2 * j:2 * j + 2, 1, :], src[:, :, 1, :], up_incl[:, kind, :], 2).then_inc(S["gram_k_taken"], 1)
                for l in range(nlev):
                    for grp in range(2):
                        n = 2 * (lev0 + l) + grp
                        qs = slice(4 * grp, 4 * grp + 4)
                        dve.wait_ge(S["r_ready"], n + 1)
                        if l:
                            dve.wait_ge(S["g_ready"], n - 1)
                        masked(Rs[:, qs, :], PS[:, 4 + grp, :].rearrange("p (q c) -> p q c", q=4), level[:, l + 1, :], 4)\
                            .then_inc(S["r_taken"], 1)
                    for grp in range(2):
                        n = 2 * (lev0 + l) + grp
                        qs = slice(4 * grp, 4 * grp + 4)
                        dve.wait_ge(S["g_ready"], n + 1)
                        dve.wait_ge(S["g_first"], t + 1)
                        tt(MtRb[:, qs, 0, :], PS[:, 6 + grp, :].rearrange("p (q c) -> p q c", q=4), MtRb[:, qs, 0, :], ALU.add)\
                            .then_inc(S["g_added"], 1)
                for c in range(1 if t == 0 else 2):
                    n = ch0 + c
                    rows = slice(64 * c, 64 * c + 64)
                    dc = 0 if t == 0 else 1 + DB + n - 1
                    dve.wait_ge(S["u_ready"], n + 1)
                    v.tensor_copy(Us[rows], PS[rows, 2, :]).then_inc(S["u_taken"], 1)
                    dve.wait_ge(S["st_ready"], n + 1)
                    for hp in range(2):
                        lo = slice(64 * hp, 64 * hp + 64)
                        src = PS[lo, 4, 0:NG * HD].rearrange("p (g i) -> p g i", g=NG)
                        ch(tt(tmpS[lo], src, ST[lo, :, lo], ALU.add))
                    ch.wait()
                    for hp in range(2):
                        lo = slice(64 * hp, 64 * hp + 64)
                        ins = tt(ST[lo, :, lo], tmpS[lo], Dc[lo, :, dc:dc + 1].to_broadcast([64, NG, HD]), ALU.mult)
                    ins.then_inc(S["st_done"], 1)
                    dve.wait_ge(S["st_done"], n + 2)
                if t == 0:
                    dve.wait_ge(S["us_ready"], 1)
                    v.tensor_copy(Us[64:P], PS[64:P, 2, :]).then_inc(S["us_taken"], 1)
                    dve.wait_ge(S["us_taken"], 1)
                    dve.wait_ge(S["y_ready"], 1)
                    for h in range(H):
                        g = h // 2
                        if h:
                            dve.wait_ge(S["sn_ready"], h)
                        for w, src in enumerate((Us, nat_[:, 3, :])):
                            s_ = src[64:P, h * HD:(h + 1) * HD].unsqueeze(1).to_broadcast([64, DB, HD])
                            ins = tt(Um[64:P, w], s_, seq_of[64:P].unsqueeze(2).to_broadcast([64, DB, HD]), ALU.mult)
                        ins.then_inc(S["um_ready"], 1)
                        if h % 2 == 0:
                            continue
                        dve.wait_ge(S["sn_ready"], h + 1)
                        for hp in range(2):
                            lo = slice(64 * hp, 64 * hp + 64)
                            ch(tt(Sn[lo, g, :].rearrange("p (b i) -> p b i", b=DB),
                                  PS[lo, 6 + g % 2, :].rearrange("p (b i) -> p b i", b=DB), S0T[lo, :, g, lo], ALU.add))
                        ch.wait()
                        sg = Sn[:, g, :].rearrange("p (b i) -> p b i", b=DB)
                        tt(sg, sg, Dc[:, g, 1:1 + DB].unsqueeze(2).to_broadcast([P, DB, HD]), ALU.mult).then_inc(S["sn_taken"], 1)
                    v.memset(small[:, 2:3], 0.0).then_inc(S["um_used"], H)
                v.memset(small[:, 3:4], 0.0).then_inc(S["prev_tile"], 1)
                dve.wait_ge(S["prev_tile"], t + 1)

            dve.wait_ge(S["y_taken"], NTILE)
            v.memset(small[:, 0:1], 0.0).then_inc(S["hs_in"], 1)
            for g in range(NG):
                n = 2 * NG + g
                dve.wait_ge(S["hs_ready"], n + 1)
                ins = stt(two(YT[:, g]), hs(n), -1.0 / HD, two(YT[:, g]), ALU.mult, ALU.add).then_inc(S["hs_taken"], 1)
            dve.wait_ge(S["hs_taken"], 3 * NG)
            v.memset(small[:, 1:2], 0.0).then_inc(S["yc_ready"], 1)
            for g in range(NG):
                n = 3 * NG + g
                dve.wait_ge(S["hs_ready"], n + 1)
                ts(two(T2[:, g]), hs(n), 1.0 / HD, GN_EPS, ALU.mult, ALU.add).then_inc(S["hs_taken"], 1)
            dve.wait_ge(S["hs_taken"], 4 * NG)
            v.memset(small[:, 1:2], 0.0).then_inc(S["root_in"], 1)
            dve.wait_ge(S["root_done"], 2)
            ch(v.reciprocal(T2, T2))
            ch.wait()
            ch(tt(YT, YT, T2, ALU.mult))
            ch.wait()
            for g in range(NG):
                ch(ts(YT[:, g], YT[:, g], pc("gn_g", g), pc("gn_b", g), ALU.mult, ALU.add))
            ch.wait()
            ch(tt(YT, YT, kk, ALU.add))
            ch.wait()
            tt(mixT[:, NG:, 0:SEQ], YT[:, :, P:TL], gate[:, :, P:TL], ALU.mult)
            tt(mixT[:, NG:, SEQ:OUTC], YT[:, :, 64:P], gate[:, :, 64:P], ALU.mult).then_inc(S["rwkv_done"], 1)
            dve.wait_ge(S["rwkv_done"], 1)
            v.memset(small[:, 5:6], 0.0).then_inc(S["k_free"], NRING)
            v.memset(small[:, 6:7], 0.0).then_inc(S["v_free"], NRING)

            dve.wait_ge(S["ln_in"], 32)
            for t in range(2):
                ch(v.tensor_reduce(tot[:, t, :], Ln[:, t, :].rearrange("p (k h) -> p h k", h=H), AX.X, ALU.add))
            ch.wait()
            for t in range(2):
                ins = tt(TU[:, t], tot[:, t, :].unsqueeze(2).to_broadcast([P, H, P]),
                         later_page.unsqueeze(1).to_broadcast([P, H, P]), ALU.mult)
            ins.then_inc(S["tu_ready"], 1)
            dve.wait_ge(S["rl_taken"], 4)
            ch(v.memset(mx[:, 64:P], 0.0))

            def add_bias(b, j):
                dve.wait_ge(S["sc_page"], b * NPG + 8 * (j + 1))
                bias = Rl[:, bass.ds(b, 1), :, 8 * j:8 * j + 8].rearrange("p o h g -> p g (o h)").unsqueeze(3)
                tt(Sb[:, 8 * j:8 * j + 8, :].rearrange("p g (h t) -> p g h t", h=H),
                   PS[:, 2 + j % 2, :].rearrange("p (g h t) -> p g h t", g=8, h=H),
                   bias.to_broadcast([P, 8, H, DS]), ALU.add).then_inc(S["sc_taken"], 1)

            def scores_of(b, prev):
                dve.wait_ge(S["new_ready"], b + 1)
                if prev:
                    dve.wait_ge(S["p_in"], b * 2)
                tt(Sb[:, NPG, :].rearrange("p (h t) -> p h t", h=H), PS[:, 6, 0:64].rearrange("p (h t) -> p h t", h=H),
                   RN[:, bass.ds(b, 1)].rearrange("p o h t -> p (o h) t"), ALU.add).then_inc(S["new_taken"], 1)
                for j in range(4):
                    add_bias(b, j)
                    if prev and j == 0:
                        sums_of(b - 1)
                    if prev and j == 1:
                        dve.wait_ge(S["sum_ready"], b)
                        v.reciprocal(rden, PS[:, 5, 0:64]).then_inc(S["rden_done"], 1)
                dve.wait_ge(S["sc_taken"], b * 4 + 4)
                dve.wait_ge(S["new_taken"], b + 1)
                v.tensor_reduce(mx[:, 0:64], Sb.rearrange("p g q -> p q g"), AX.X, ALU.max).then_inc(S["mx_in"], 1)
                if prev:
                    output_of(b - 1)
                dve.wait_ge(S["mx_turned"], b + 1)
                v.tensor_reduce(m1[0:64], PS[0:64, 7, 0:P], AX.X, ALU.max).then_inc(S["m1_done"], 1)
                dve.wait_ge(S["m1_done"], b + 1)
                ts(dg[0:64, :], ident[0:64, 0:64], m1[0:64], None, ALU.mult).then_inc(S["dg_ready"], 1)
                dve.wait_ge(S["mx_spread"], b + 1)
                mb = PS[:, 7, P:P + 64].unsqueeze(1)
                tt(Pb[:, 0:16, :], Sb[:, 0:16, :], mb.to_broadcast([P, 16, 64]), ALU.subtract).then_inc(S["p_in"], 1)
                tt(Pb[:, 16:NPG + 1, :], Sb[:, 16:NPG + 1, :], mb.to_broadcast([P, 17, 64]), ALU.subtract).then_inc(S["p_in"], 1)

            def sums_of(b):
                dve.wait_ge(S["exp_out"], b * 2 + 2)
                v.tensor_reduce(sm, Pb.rearrange("p g q -> p q g"), AX.X, ALU.add).then_inc(S["sm_ready"], 1)

            def output_of(b):
                dve.wait_ge(S["v_free"], NRING + NPG + b * NPG)
                dve.wait_ge(S["rden_done"], b + 1)
                for hp in range(2):
                    lo = slice(64 * hp, 64 * hp + 64)

                    def own(w):
                        return w.rearrange("p (g n) -> p g n", g=NG)[lo, :, 8 * hp:8 * hp + 8]

                    ins = tt(mixT[lo, 0:NG, bass.ds(SEQ + b * DS, DS)], own(PS[:, 4, 0:64]), own(rden), ALU.mult)
                ins.then_inc(S["o_done"], 1)

            scores_of(0, False)
            with dve.Fori(1, DB) as b:
                scores_of(b, True)
            sums_of(DB - 1)
            dve.wait_ge(S["sum_ready"], DB)
            dve.wait_ge(S["o_done"], DB - 1)
            v.reciprocal(rden, PS[:, 5, 0:64]).then_inc(S["rden_done"], 1)
            output_of(DB - 1)
            dve.wait_ge(S["o_done"], DB)
            dve.wait_ge(S["sm_ready"], DB)
            v.memset(small[:, 4:5], 0.0).then_inc(S["attn_done"], 1)

            order = [1, 2, 3, 4, 0]

            def rows_of(i):
                return (slice(64, P), slice(SEQ, OUTC)) if i == 0 else (slice(0, P), slice((i - 1) * P, i * P))

            def root(n, i, turn):
                rows, _ = rows_of(i)
                k = (turn + 1) * NTILE + n + 1
                dve.wait_ge(S["square_done"], k)
                ts(rstd[rows, i:i + 1], rstd[rows, i:i + 1], 1.0 / D, RMS_EPS, ALU.mult, ALU.add).then_inc(S["var_done"], 1)
                dve.wait_ge(S["std_done"], k)
                ch(v.reciprocal(rstd[rows, i:i + 1], ss[rows, i:i + 1]))
                ch.wait()

            for n in range(NTILE + 2):
                if n < NTILE:
                    i = order[n]
                    rows, _ = rows_of(i)
                    dve.wait_ge(S["mixed_out"], n + 1)
                    dve.wait_ge(x_in[i], 64 if i == 0 else 32)
                    xv = x[rows, i, :].rearrange("p (a b) -> p a b", a=2)
                    tt(xv, PS[rows, 2 * (n % 2):2 * (n % 2) + 2, :], xv, ALU.add).then_inc(S["h_ready"], 1)
                if 1 <= n <= NTILE:
                    m, i = n - 1, order[n - 1]
                    rows, _ = rows_of(i)
                    root(m, i, 0)
                    dve.wait_ge(S["h_ready"], m + 1)
                    if m >= 2:
                        dve.wait_ge(S["xT_turned"], NTILE + m - 1)
                    ts(xs2[rows, m % 2, :], x[rows, i, :], rstd[rows, i:i + 1], None, ALU.mult).then_inc(S["xs_ready"], 1)
                if n >= 2:
                    m = n - 2
                    rows, cols = rows_of(order[m])
                    w = cols.stop - cols.start
                    dve.wait_ge(S["xT_turned"], NTILE + m + 1)
                    for hf in range(2):
                        gain = par[:, pcol["ln2_g"] + 4 * hf:pcol["ln2_g"] + 4 * hf + 4].unsqueeze(2)
                        src = PS[:, 4 + 2 * (m % 2) + hf, 0:4 * w].rearrange("p (f c) -> p f c", c=w)
                        ins = tt(hT[:, 4 * hf:4 * hf + 4, cols], src, gain.to_broadcast([P, 4, w]), ALU.mult)
                    ins.then_inc(S["xnT_ready"], 1)
            HO = OUTC // 2
            for f in range(NF):
                dve.wait_ge(S["silu_done"], f + 1)
                tt(actT[:, f, :].rearrange("p (a b) -> p a b", a=2), PS[:, 4 * (f % 2) + 2:4 * (f % 2) + 4, 0:HO],
                   sgate[:, f % 2, :].rearrange("p (a b) -> p a b", a=2), ALU.mult).then_inc(S["act_ready"], 1)
            for half in range(2):
                for n, i in enumerate(order):
                    rows, _ = rows_of(i)
                    if n < NTILE - 1:
                        dve.wait_ge(S["down_tile"], (NTILE - 1) * half + n + 1)
                    else:
                        dve.wait_ge(S["down_used"], 3 * (half + 1))
                    xv = x[rows, i, half * NB:(half + 1) * NB]
                    tt(xv, PS[rows, (5 * half + n) % 8, :], xv, ALU.add).then_inc(S["h_ready"] if half else S["down_taken"], 1)
            dve.wait_ge(S["lnf_in"], 16)
            for n, i in enumerate(order):
                rows, _ = rows_of(i)
                root(n, i, 1)
                dve.wait_ge(S["down_taken"], NTILE)
                stt(x[rows, i, :], x[rows, i, :], rstd[rows, i:i + 1], lnf[rows], ALU.mult, ALU.mult).then_inc(S["y_final"], 1)

        assert N_OUT_DMA[0] == N_FIRST_OUT + NTILE

        @block.sync
        def _(sp):
            sp.wait_ge(S["out_done"], 16 * N_OUT_DMA[0])
            for n in range(2):
                sp.wait_ge(S[f"so_out{n}"], 64)
            sp.wait_ge(S["fs_out"], 32)


_OUTS = [("y_prompt", (1, SEQ, D)), ("y_sample", (DB, DS, D)), ("k_prompt", (1, 1, NPT, H, HD)), ("v_prompt", (1, 1, NPT, H, HD)),
         ("logf_prompt", (1, 1, NPT, H)), ("wkv_prompt", (1, 1, H, HD, HD)), ("shift_prompt", (1, 1, D)),
         ("k_sample", (1, DB, DS, H, HD)), ("v_sample", (1, DB, DS, H, HD)), ("logf_sample", (1, DB, DS, H)),
         ("wkv_sample", (1, DB, H, HD, HD)), ("shift_sample", (1, DB, D))]


def kernel(**inputs):
    import numpy as _np
    import concourse.bacc as _bacc
    from concourse import mybir as _mybir
    from concourse.bass_utils import run_bass_kernel_spmd as _run

    nc = _bacc.Bacc("TRN2", target_bir_lowering=False, num_devices=1)
    arrays, t_in, t_out = {}, {}, {}
    for name, a in inputs.items():
        a = _np.ascontiguousarray(a)
        arrays[f"in_{name}"] = a
        t_in[name] = nc.dram_tensor(f"in_{name}", a.shape, _mybir.dt.from_np(a.dtype), kind="ExternalInput").ap()
    for name, shape in _OUTS:
        t_out[name] = nc.dram_tensor(f"out_{name}", shape, _mybir.dt.float32, kind="ExternalOutput").ap()
    build(nc, t_in, t_out)
    r = _run(nc, [arrays], core_ids=[0])
    return tuple(r.results[0][f"out_{name}"] for name, _ in _OUTS)
```

```python
from contextlib import ExitStack

import concourse.bass as bass
from concourse import mybir

F32 = mybir.dt.float32
I32 = mybir.dt.int32
ALU = mybir.AluOpType
ACT = mybir.ActivationFunctionType
AX = mybir.AxisListType

P = 128
D = 1024
KT = D // P
NMETA = 16
SEQ = 512
NPT = NMETA + SEQ
DB = 8
DS = 8
NS = DB * DS
H = 8
HD = 64
NG = H * HD // P
FOXW = H * HD
FOXC = 3 * FOXW + H
DFF = 2816
NF = DFF // P
NTILE = 5
RAW = 602
RS0 = 1 + NPT
TL = NTILE * P
OUTC = SEQ + NS
PAGE = 128
NPG = 32
NB = 512
NEG = -1.0e30
RMS_EPS = 1e-6
GN_EPS = 64e-5
E_HALF = 0.6065306597126334
PAR_ROWS = [("ln1_g", 8), ("mu_shift", 14), ("w0", 4), ("a0", 4), ("k_k", 4), ("k_a", 4), ("r_k", 4), ("gn_g", 4),
            ("gn_b", 4), ("ln2_g", 8)]
NPAR = sum(n for _, n in PAR_ROWS)


class Chain:

    def __init__(self, eng, sem):
        self.eng, self.sem, self.n = eng, sem, 0

    def __call__(self, ins):
        ins.then_inc(self.sem, 1)
        self.n += 1
        return ins

    def wait(self):
        self.eng.wait_ge(self.sem, self.n)


def build(nc, t_in, t_out):
    ctx = ExitStack()
    with ctx:
        def sem(name):
            return ctx.enter_context(nc.semaphore(name))

        arena = ctx.enter_context(nc.sbuf_tensor("arena", [P, 52800], F32))
        PS = ctx.enter_context(nc.psum_tensor("PS", [P, 8, NB], F32))
        ptab = ctx.enter_context(nc.sbuf_tensor("ptab", [1, DB * NPG], I32))
        top = [0]

        def at(off, *dims):
            n = 1
            for d in dims:
                n *= d
            v = arena[:, off:off + n]
            if len(dims) == 2:
                v = v.rearrange("p (a b) -> p a b", a=dims[0])
            elif len(dims) == 3:
                v = v.rearrange("p (a b c) -> p a b c", a=dims[0], b=dims[1])
            elif len(dims) == 4:
                v = v.rearrange("p (a b c d) -> p a b c d", a=dims[0], b=dims[1], c=dims[2])
            return v

        def new(*dims):
            n = 1
            for d in dims:
                n *= d
            off = top[0]
            top[0] += n
            assert top[0] <= 52800, top[0]
            return at(off, *dims)

        ident = new(P)
        ones = new(P)
        headones = new(P)
        sel = new(H, P)
        causal = new(P)
        level = new(6, P)
        up_incl = new(2, P)
        up_strict = new(2, P)
        low_strict = new(2, P)
        spread = new(P)
        later_page = new(P)
        chunk_mask = new(TL)
        forget_mask = new(RAW)
        par = new(NPAR)
        ss, rstd = new(NTILE), new(NTILE)
        bf_col = new(1)
        small = new(8)
        RN = new(DB, H, DS)
        cnat = new(H)
        seq_of = new(DB)
        Dc = new(NG, 1 + DB + SEQ // 64)
        kTS = new(NG, P)
        lognat = new(NTILE, H)
        QB = new(DB, NG, 16)
        MIX0 = top[0]
        mixT = new(2 * NG, OUTC)
        qT_off = top[0]
        kT = new(NG, RAW)
        qT = new(NG, RAW)
        vnat = new(NTILE, FOXW)
        FREE = top[0]
        x = new(NTILE, D)
        B0 = top[0]

        pcol = {}
        at_row = 0
        for name, n in PAR_ROWS:
            pcol[name] = at_row
            at_row += n

        def pc(name, i, lo=0, hi=P):
            return par[lo:hi, pcol[name] + i:pcol[name] + i + 1]

        top[0] = B0
        xnT = new(KT, RAW)
        wring = new(2, KT, 520)
        XR = new(14, TL)
        xs = at(MIX0, 2, D)
        xsq = at(MIX0 + 2 * D, D)
        raw = new(2, RAW)
        diff = new(RAW)
        parn = at(MIX0 + 3 * D, P)
        kn = new(NTILE, FOXW)
        fT = new(RAW)
        f2 = at(MIX0 + 3 * D + P, RAW)
        xnS = at(MIX0 + 3 * D + P + RAW, KT, NS)
        assert 3 * D + P + RAW + KT * NS <= 2 * NG * OUTC
        cT = new(RAW)
        LT = new(TL)
        shn = new(D)
        END1 = top[0]

        top[0] = B0
        NCB = new(H, NPT)
        Sp = new(3, 544)
        PT = new(2, NTILE, P)
        mxp, nmp, smp, rcp = new(3), new(3), new(3), new(3)
        assert top[0] <= B0 + KT * RAW + 2 * KT * 520

        names = """consts x0_zeroed par_in par_turned par_ready square_done var_done std_done xs_ready xT_turned
        xnT_ready w_landed0 w_landed1 proj_ready proj_taken nat_ready nat_taken mixed_done f_in logf_a log_ready
        ncb_ready ncb_taken s_ready s_added mx_ready exp_done p_ready pt_ready pt_taken pv_ready o_taken out_done
        qb_ready kts_ready act_c dve_c pool_c pt_zero shn_turned shn_ready
        lr_in lr_act lr_ready lr_taken hs_in hs_ready hs_rows hs_taken pre_done L_ready decays root_in root_done
        turned turned_taken gram_b gram_b_taken gram_m gram_k gram_k_taken g_first x_turned x_taken r_ready r_taken g_ready g_added
        nv_ready nv_taken wt_ready wt_taken st_done u_ready u_taken st_ready s0_in0 s0_in1 s0_turned s0_taken ut_ready ut_taken
        us_ready us_taken y_ready y_taken um_ready um_used sn_ready sn_taken so_turned so_taken so_out0 so_out1 fs_turned
        fs_taken fs_out yc_ready rwkv_done prev_tile
        ptab_in k_free v_free attn_done wo_in gu_ready down_used ln_in y_final 
        kt_taken sc_taken sc_page new_ready new_taken 
        exp_out mixed_out h_ready act_ready down_tile down_taken 
        silu_done o_done later_sum tot_ready rt_ready rt_stored r_in0 r_in1
        rn_padded rn_turned rn_taken qc_ready max_steps mxg_done pr_turned pr_taken prn_turned prn_taken o_scaled o_turned sum_steps""".split()
        S = {n: sem(n) for n in names}
        X0 = FREE
        WA = at(X0, FOXW)
        G2 = at(X0 + FOXW, FOXW)
        MtRb = at(X0, H, 2, P)
        NtRk = at(X0 + 2048, H, 2, P)
        Ms = at(X0 + 4096, H, P)
        AR = at(B0, 2, NG, TL)
        Kd = at(B0 + 5120, NG, TL)
        Bd = at(B0 + 7680, NG, TL)
        gate = at(B0 + 10240, NG, TL)
        assert 12800 <= KT * RAW + 2 * KT * 520
        XR0 = B0 + KT * RAW + 2 * KT * 520
        HI = XR0 + 14 * TL
        kk = at(HI, NG, TL)
        T2 = at(HI + 2560, NG, TL)
        Rn = T2[:, 0]
        nat_ = at(HI + 2560, 4, FOXW)
        Xs = at(HI + 2560 + 2048, H, P)
        NVs = at(HI + 2560 + 3072, FOXW)
        Wt = at(HI + 2560 + 3584, NG, P)
        Us = at(HI + 2560 + 4096, FOXW)
        assert HI + 2560 + 4608 <= 52800, HI
        YT = at(XR0, NG, TL)
        S0n = at(XR0 + 2560, DB // 2, NG, P)
        ST = at(XR0 + 2560 + 2048, NG, P)
        Rs = at(XR0 + 12 * TL, H, P)
        S0T = at(qT_off, DB, NG, P)
        tmpS = at(qT_off + 4096, NG, HD)
        Sn = S0n.rearrange("p a b c -> p (a b c)").rearrange("p (g n) -> p g n", g=NG)
        SOo = at(X0 + 2048, 2, DB, P)
        Um = at(X0, 2, DB, HD)
        UTs = Rs.rearrange("p a b -> p (a b)")[:, 0:NG * NS].rearrange("p (g n) -> p g n", g=NG)
        NRING = 16
        LOT = 4
        top[0] = B0
        Kr = new(NRING, FOXW)
        Vr = new(NRING, FOXW)
        KTs = new(2, NG, P)
        Pb = new(NPG + 1, P)
        Rr = new(NPG, P)
        RNT = new(DB, P)
        PTs = new(2, LOT, P)
        PTn = new(P)
        Qc = new(NG, 32)
        Oc = new(P)
        mxg = new(NPG // LOT + 1)
        m1, nm, rs, rden = new(1), new(1), new(1), new(1)
        NEXP = 3
        ss3 = new(NEXP)
        pidx = at(52800 - 2, 2).bitcast(I32)
        assert top[0] <= 52800, top[0]
        Sb = at(qT_off, NPG + 1, P)
        Ln = at(qT_off, 2, PAGE * H)
        Rt = at(qT_off + 2 * PAGE * H, 2, H, PAGE)
        RNp = at(X0, DB, NG, 32)
        assert 4 * PAGE * H <= DB * NG * P and (NPG + 1) * P <= 2 * NG * RAW
        NLOT = NPG // LOT
        ROWS = [slice(32 * g, 32 * g + 32) for g in range(NG)]
        forgets_after = nc.dram_tensor("forgets_after", (DB, H, NPG * PAGE), F32, kind="Internal")
        hT = at(qT_off, KT, OUTC)
        sgate = at(qT_off + KT * OUTC, 2, OUTC)
        assert KT * OUTC + 2 * OUTC <= X0 - qT_off
        xs2 = at(X0 - 2 * D, 2, D)
        assert 2 * D <= (NTILE - 1) * FOXW
        xsq2 = at(52800 - D, D)
        assert top[0] <= 52800 - D
        top[0] = B0
        actT = new(NF, OUTC)
        wo = at(B0, KT, D)
        FR = 3
        top[0] = B0 + 2 * NRING * FOXW + 2 * NG * P + (NPG + 1) * P - 2 * 4096
        assert top[0] >= B0 + NF * OUTC
        fring = new(FR, 4096)
        lnf = new(D)
        assert top[0] <= 52800 - D
        assert top[0] <= 52800
        x_in = [sem(f"x_in{i}") for i in range(NTILE)]

        k_in = [sem(f"k_in{i}") for i in range(NRING // LOT)]
        v_in = [sem(f"v_in{i}") for i in range(NRING // LOT)]
        f_in = [sem(f"f_in{i}") for i in range(FR)]
        block = ctx.enter_context(nc.Block())

        WCH = [(0, 512), (512, 512), (1024, 520), (1544, 512), (2056, 512), (2568, 512), (3080, 256)]
        w_in = t_in["w_in"]
        ITEMS = [(0, g * P, P, ("q", g)) for g in range(NG)] + [(1, g * P, P, ("k", g)) for g in range(NG)] + \
            [(2, 512, H, ("f", 0))] + \
            [(3 + c, g * P, P, ("rw", 4 * c + g)) for c in range(3) for g in range(NG)] + \
            [(6, 0, P, ("rw", 12)), (6, P, P, ("rw", 13))]
        HALF = RAW // 2
        NRW0 = 9
        N_OUT_DMA = [0]
        N_FIRST_OUT = 11

        def samp(v, first):
            return v[:, RS0:RS0 + 9 * DB].rearrange("p (b n) -> p b n", n=9)[:, :, first:first + DS]

        def samps(v):
            return v[:, :, RS0:RS0 + 9 * DB].rearrange("p k (b n) -> p k b n", n=9)[:, :, :, 1:9]

        def out_dma(eng, dst, src):
            N_OUT_DMA[0] += 1
            eng.dma_start(dst, src).then_inc(S["out_done"], 16)

        @block.sync
        def _(sp):
            for name, n in PAR_ROWS:
                src = t_in[name]
                if name == "r_k":
                    src = src[0].rearrange("h d -> (h d)").rearrange("(a p) -> a p", p=P)
                elif name in ("lnf_g",):
                    src = src.rearrange("(a p) -> a p", p=P)
                else:
                    src = src[0].rearrange("(a p) -> a p", p=P)
                r = pcol[name]
                sp.dma_start(parn[r:r + n, :], src).then_inc(S["par_in"], 16)
            sp.dma_start(bf_col[0:H, :], t_in["b_f"].rearrange("o h -> h o")).then_inc(S["f_in"], 16)
            sp.wait_ge(S["x0_zeroed"], 1)
            sp.dma_start(x[0:NMETA, 0, :], t_in["meta_tokens"]).then_inc(x_in[0], 16)
            sp.dma_start(x[32:32 + DB, 0, :], t_in["state_shift"][0]).then_inc(x_in[0], 16)
            sp.dma_start(x[64:P, 0, :], t_in["x_sample"].rearrange("b t d -> (b t) d")).then_inc(x_in[0], 16)
            for i in range(1, NTILE):
                sp.dma_start(x[:, i, :], t_in["x_prompt"][0, (i - 1) * P:i * P, :]).then_inc(x_in[i], 16)
            for c, (c0, n) in enumerate(WCH):
                if c >= 2:
                    sp.wait_ge(S["proj_ready"], sum(1 for it in ITEMS if it[0] <= c - 2))
                    if c - 2 == 2:
                        sp.wait_ge(S["nat_ready"], NTILE)
                sp.dma_start(wring[:, c % 2, :, 0:n],
                             w_in[0].rearrange("(k p) n -> p k n", p=P)[:, :, c0:c0 + n]).then_inc(S[f"w_landed{c % 2}"], 16)

            sp.wait_ge(S["xs_ready"], NTILE)
            sp.dma_start(WA[0:64, :], t_in["w2"][0]).then_inc(S["lr_in"], 16)
            sp.dma_start(WA[64:P, :], t_in["a2"][0]).then_inc(S["lr_in"], 16)
            sp.dma_start(G2, t_in["g2"][0]).then_inc(S["lr_in"], 16)
            sp.wait_ge(S["pre_done"], 1)
            for b in range(DB):
                if b == DB // 2:
                    sp.wait_ge(S["s0_turned"], DB // 2)
                for hp in range(2):
                    lo = slice(64 * hp, 64 * hp + 64)
                    src = t_in["state_wkv"][0, b].rearrange("(g a) i j -> a i g j", a=2)[hp]
                    sp.dma_start(S0n[lo, b % (DB // 2), :, lo], src).then_inc(S[f"s0_in{2 * b // DB}"], 16)
            sp.dma_start(ptab[:, :], t_in["page_table"].rearrange("b p -> (b p)").unsqueeze(0)).then_inc(S["ptab_in"], 16)
            sp.wait_ge(S["ptab_in"], 16)
            n_pool = t_in["cache_k"].shape[1]
            k_pages = t_in["cache_k"][0].rearrange("n p h d -> n p (h d)")
            v_pages = t_in["cache_v"][0].rearrange("n p h d -> n p (h d)")

            def page_numbers(b, p0):
                _, numbers = nc.values_load_multi_w_load_instructions(
                    ptab[0:1, bass.ds(b * NPG + p0, LOT)], engines=(mybir.EngineType.SP,), min_val=0, max_val=n_pool - 1,
                    skip_runtime_bounds_check_because="a page table holds numbers of pages of the pool", bass_reorder=False)
                return numbers

            def load_lot(pages, ring, free, landed, numbers, b, p0):
                sp.wait_ge(S[free], b * NPG + (p0 + LOT))
                for p, page in zip(range(p0, p0 + LOT), numbers):
                    sp.dma_start(ring[:, p % NRING, :], pages[bass.ds(page, 1)].rearrange("o p n -> p (o n)"))\
                        .then_inc(landed[p % NRING // LOT], 16)

            for p0 in range(0, NPG, LOT):
                load_lot(k_pages, Kr, "k_free", k_in, page_numbers(0, p0), 0, p0)
            with sp.Fori(1, DB) as b:
                for p0 in range(0, NPG, LOT):
                    load_lot(k_pages, Kr, "k_free", k_in, page_numbers(b, p0), b, p0)
                    load_lot(v_pages, Vr, "v_free", v_in, page_numbers(b - 1, p0), b - 1, p0)
            sp.wait_ge(S["k_free"], NRING + DB * NPG)
            sp.dma_start(wo, t_in["w_out"][0].rearrange("(k p) n -> p k n", p=P)).then_inc(S["wo_in"], 16)
            for p0 in range(0, NPG, LOT):
                load_lot(v_pages, Vr, "v_free", v_in, page_numbers(DB - 1, p0), DB - 1, p0)
                i = p0 // LOT + 1
                if i < NTILE:
                    sp.dma_start(x[:, i, :], t_in["x_prompt"][0, (i - 1) * P:i * P, :]).then_inc(x_in[i], 16)
            sp.dma_start(x[64:P, 0, :], t_in["x_sample"].rearrange("b t d -> (b t) d")).then_inc(x_in[0], 16)
            sp.wait_ge(S["sc_taken"], DB * NLOT)
            for r in range(17):
                slot = fring[:, (r + 2) % FR, :]
                if r == 1:
                    sp.wait_ge(S["attn_done"], 1)
                    sp.dma_start(lnf, t_in["lnf_g"].partition_broadcast(P)).then_inc(S["wo_in"], 16)
                if r >= FR:
                    if r - FR < 11:
                        sp.wait_ge(S["gu_ready"], 2 * (r - FR + 1))
                    else:
                        sp.wait_ge(S["down_used"], r - FR - 10)
                if r < 11:
                    for w, name in enumerate(("w_gate", "w_up")):
                        sp.dma_start(slot[:, w * 2048:(w + 1) * 2048].rearrange("p (k n) -> p k n", k=KT),
                                     t_in[name][0].rearrange("(k p) n -> p k n", p=P)[:, :, r * 256:(r + 1) * 256])\
                            .then_inc(f_in[r % FR], 16)
                else:
                    half, c = (r - 11) // 3, (r - 11) % 3
                    n0, n1 = 8 * c, min(8 * c + 8, NF)
                    sp.dma_start(slot[:, 0:(n1 - n0) * NB].rearrange("p (k n) -> p k n", n=NB),
                                 t_in["w_down"][0].rearrange("(k p) n -> p k n", p=P)[:, n0:n1, half * NB:(half + 1) * NB])\
                        .then_inc(f_in[r % FR], 32)

        @block.gpsimd
        def _(pool):
            chain = Chain(pool, S["pool_c"])
            g = nc.gpsimd
            g.memset(x[:, 0, :], 0.0).then_inc(S["x0_zeroed"], 1)
            pool.wait_ge(S["x0_zeroed"], 1)

            def ch(ins):
                chain(ins)
                chain.wait()

            def keep(v, pattern, base, cm, fill=0.0):
                ch(g.affine_select(out=v, in_=v, compare_op=ALU.is_ge, fill=fill, base=base, pattern=pattern,
                                   channel_multiplier=cm))

            ch(g.memset(ident, 0.0))
            ch(g.affine_select(out=ident, in_=ident, compare_op=ALU.not_equal, fill=1.0, base=0, pattern=[[-1, P]],
                               channel_multiplier=1))
            g.memset(small, 0.0).then_inc(S["consts"], 1)
            pool.wait_ge(S["consts"], 1)
            ch(g.memset(ones, 1.0))
            ch(g.memset(headones, 0.0))
            for q in range(2):
                ch(g.memset(headones[64 * q:64 * q + 64, 64 * q:64 * q + 64], 1.0))
            ch(g.memset(sel, 0.0))
            ch(g.affine_select(out=sel, in_=sel, compare_op=ALU.not_equal, fill=1.0, base=0, pattern=[[-1, H], [0, P]],
                               channel_multiplier=1))
            ch(g.memset(causal, 0.0))
            keep(causal, [[-1, P]], 0, 1, NEG)
            ch(g.memset(level, 0.0))
            for l in range(6):
                n = 2 << l
                v = level[:, l, :].rearrange("p (a c) -> p a c", c=n)[:, :, n // 2:n]
                ch(g.memset(v, 1.0))
                keep(v, [[-n, P // n], [0, n // 2]], 0, 1)
                keep(v, [[n, P // n], [0, n // 2]], n // 2 - 1, -1)
            for kind in range(2):
                for m, off in ((up_incl, 0), (up_strict, -1)):
                    v = m[:, kind, :]
                    ch(g.memset(v, 1.0))
                    keep(v, [[1, P]], off, -1)
                    keep(v, [[-64, 2], [0, 64]], 0, 1)
                    if kind == 0:
                        keep(v[:, 64:P], [[-DS, DB], [0, DS]], -64, 1)
                v = low_strict[:, kind, :]
                ch(g.memset(v, 1.0))
                keep(v, [[-1, P]], -1, 1)
                keep(v, [[64, 2], [0, 64]], 63, -1)
                if kind == 0:
                    keep(v[:, 64:P], [[DS, DB], [0, DS]], 64 + DS - 1, -1)
            for v, n in ((later_page, NPG),):
                ch(g.memset(v, 1.0))
                keep(v, [[-1, P]], -1, 1)
                if n < P:
                    keep(v, [[n, P // n], [0, n]], n - 1, -1)
            ch(g.memset(spread, 0.0))
            for q in range(2 * NG):
                v = spread[:, 64 * (q % 2):64 * (q % 2) + 64]
                ch(g.affine_select(out=v, in_=v, compare_op=ALU.not_equal, fill=1.0, base=-16 * q, pattern=[[0, 64]],
                                   channel_multiplier=1))
            ch(g.memset(chunk_mask, 1.0))
            ch(g.memset(forget_mask, 1.0))
            ch(g.memset(chunk_mask[:, 0:1], 0.0))
            ch(g.memset(chunk_mask[:, 64:P].rearrange("p (b t) -> p b t", t=DS)[:, :, 0:1], 0.0))
            ch(g.memset(chunk_mask[:, P:TL].rearrange("p (c t) -> p c t", t=64)[:, :, 0:1], 0.0))
            ch(g.memset(forget_mask[:, 0:2], 0.0))
            ch(g.memset(forget_mask[:, RS0:RS0 + 9 * DB].rearrange("p (b n) -> p b n", n=9)[:, :, 0:2], 0.0))
            ch(g.memset(RN, 0.0))
            keep(RN, [[-DS, DB], [0, H], [0, DS]], -64, 1, NEG)
            keep(RN, [[DS, DB], [0, H], [1, DS]], 64, -1, NEG)
            ch(g.memset(seq_of, 1.0))
            keep(seq_of, [[-DS, DB]], -64, 1)
            keep(seq_of, [[DS, DB]], 64 + DS - 1, -1)
            ch(g.memset(xnT[:, :, 0:1], 0.0))
            ch(g.memset(xnT[:, :, RAW - 1:RAW], 0.0))
            ch(g.memset(XR[:, :, NMETA:64], 0.0))
            ch(g.memset(vnat[:, 0, :], 0.0))
            ch(g.memset(LT, 0.0))
            ch(g.memset(QB, 0.0))
            g.memset(kTS[:, :, 0:64], 0.0).then_inc(S["consts"], 1)
            k_out, v_out = t_out["k_prompt"][0, 0], t_out["v_prompt"][0, 0]
            pool.wait_ge(S["nat_taken"], 12)
            flat = "t h d -> t (h d)"
            for dst, src in ((k_out, kn), (v_out, vnat)):
                dst = dst.rearrange(flat)
                out_dma(pool, dst[0:NMETA, :], src[0:NMETA, 0, :])
                out_dma(pool, dst[NMETA:NPT, :].rearrange("(i p) n -> p i n", p=P), src[:, 1:5, :])
            out_dma(pool, t_out["k_sample"][0].rearrange("b t h d -> (b t) (h d)"), kn[64:P, 0, :])
            out_dma(pool, t_out["v_sample"][0].rearrange("b t h d -> (b t) (h d)"), vnat[64:P, 0, :])
            lf = t_out["logf_prompt"][0, 0]
            out_dma(pool, lf[0:NMETA, :], lognat[0:NMETA, 0, :])
            out_dma(pool, lf[NMETA:NPT, :].rearrange("(i p) n -> p i n", p=P), lognat[:, 1:5, :])
            out_dma(pool, t_out["logf_sample"][0].rearrange("b t h -> (b t) h"), lognat[64:P, 0, :])
            pool.wait_ge(S["shn_ready"], 1)
            out_dma(pool, t_out["shift_prompt"][0], shn[0:1, :])
            out_dma(pool, t_out["shift_sample"][0], shn[1:1 + DB, :])
            w_out_ = t_out["wkv_sample"][0]
            for g in range(NG):
                pool.wait_ge(S["so_taken"], g + 1)
                for hp in range(2):
                    N_OUT_DMA[0] += 0
                    pool.dma_start(w_out_[:, 2 * g + hp].rearrange("b i j -> i b j"), SOo[0:64, g % 2, :, 64 * hp:64 * hp + 64])\
                        .then_inc(S[f"so_out{g % 2}"], 16)
            pool.wait_ge(S["sn_taken"], NG)
            with nc.allow_non_contiguous_dma(reason="256 page numbers"):
                pool.dma_start(pidx, t_in["page_table"].rearrange("(t b) p -> (b p) t", t=2)).then_inc(S["ln_in"], 16)
            pool.wait_ge(S["ln_in"], 16)
            for t in range(2):
                nc.gpsimd.indirect_dma_start(
                    Ln[:, t, :], None, t_in["cache_logf"][0].rearrange("n p h -> n (p h)"),
                    bass.IndirectOffsetOnAxis(pidx[:, t:t + 1], 0)).then_inc(S["ln_in"], 16)
            pool.wait_ge(S["rt_ready"], 1)
            for b in range(DB):
                pool.dma_start(forgets_after[b].rearrange("h (c k) -> c h k", k=PAGE),
                               Rt[NPG * (b % 4):NPG * (b % 4 + 1), b // 4]).then_inc(S["rt_stored"], 16)

            pool.wait_ge(S["fs_taken"], 1)
            wp = t_out["wkv_prompt"][0, 0].rearrange("(g a) i j -> a i g j", a=2)
            for hp in range(2):
                lo = slice(64 * hp, 64 * hp + 64)
                pool.dma_start(wp[hp], Xs[lo, 0:NG, lo]).then_inc(S["fs_out"], 16)

            pool.wait_ge(S["rt_stored"], 16 * DB)
            pool.wait_ge(S["v_free"], NRING)

            def load_sums(b, half):
                n = NPG * PAGE // 2
                for gp in range(NG):
                    for a in range(2):
                        src = forgets_after[bass.ds(b, 1), 2 * gp + a, half * n:(half + 1) * n] if not isinstance(b, int) else \
                            forgets_after[b:b + 1, 2 * gp + a, half * n:(half + 1) * n]
                        r = 32 * gp + DS * a
                        pool.dma_start(Rr[r:r + DS, half * NPG // 2:(half + 1) * NPG // 2, :].rearrange("p a b -> p (a b)"),
                                       src.to_broadcast([DS, n])).then_inc(S[f"r_in{half}"], 16)

            load_sums(0, 0)
            load_sums(0, 1)
            with pool.Fori(1, DB) as b:
                for half in range(2):
                    pool.wait_ge(S["sc_taken"], b * NLOT + (half + 1) * NLOT // 2 - NLOT)
                    load_sums(b, half)
            for n, i in enumerate([1, 2, 3, 4, 0]):
                pool.wait_ge(S["y_final"], n + 1)
                if i == 0:
                    out_dma(pool, t_out["y_sample"].rearrange("b t d -> (b t) d"), x[64:P, 0, :])
                else:
                    out_dma(pool, t_out["y_prompt"][0, (i - 1) * P:i * P, :], x[:, i, :])

        @block.tensor
        def _(pe):
            mm = nc.tensor.matmul
            tr = nc.tensor.transpose
            pe.wait_ge(S["consts"], 1)
            pe.wait_ge(S["par_in"], 16 * len(PAR_ROWS))
            tr(PS[:, 7, 0:NPAR], parn[0:NPAR, :], ident[0:NPAR, 0:NPAR]).then_inc(S["par_turned"], 1)
            for i in range(NTILE):
                pe.wait_ge(S["xs_ready"], i + 1)
                if i >= 2:
                    pe.wait_ge(S["xnT_ready"], i - 1)
                for f in range(KT):
                    ins = tr(PS[:, 2 * (i % 2) + f // 4, (f % 4) * P:(f % 4 + 1) * P], xs[:, i % 2, f * P:(f + 1) * P], ident)
                ins.then_inc(S["xT_turned"], 1)
            pe.wait_ge(S["xnT_ready"], NTILE)
            pe.wait_ge(S["par_ready"], 1)

            nat = [0]

            def nat_slot():
                n = nat[0]
                if n >= 2:
                    pe.wait_ge(S["nat_taken"], n - 1)
                nat[0] += 1
                return PS[:, 6 + n % 2, :]

            def k_rows():
                pe.wait_ge(S["proj_taken"], 2 * NG)
                pe.wait_ge(S["kts_ready"], 1)
                for j in range(6):
                    o = nat_slot()
                    n = (NMETA, P, P, P, P, NS)[j]
                    for g in range(NG):
                        src = kT[:, g, 1:1 + NMETA] if j == 0 else kTS[:, g, 64:P] if j == 5 else \
                            kT[:, g, 17 + P * (j - 1):17 + P * j]
                        ins = tr(o[0:n, g * P:(g + 1) * P], src, ident)
                    ins.then_inc(S["nat_ready"], 1)

            def v_rows():
                for i in range(NTILE):
                    o = nat_slot()
                    parts = [(o, 17 + P * (i - 1), P)] if i else [(o[0:NMETA], 1, NMETA), (o[64:P], None, NS)]
                    for dst, c0, n in parts:
                        for k in range(KT):
                            src = xnS[:, k, :] if c0 is None else xnT[:, k, c0:c0 + n]
                            ins = mm(dst, src, wring[:, 0, k, 0:FOXW], start=(k == 0), stop=(k == KT - 1))
                    ins.then_inc(S["nat_ready"], 1)

            pe.wait_ge(S["consts"], 2)
            for f in range(KT):
                ins = tr(PS[0:9, f // 4 * 1 + 4, (f % 4) * P:(f % 4 + 1) * P], xnT[:, f, 528:601:9], ident)
            ins.then_inc(S["shn_turned"], 1)
            seen = -1
            for n, (c, c0, width, dest) in enumerate(ITEMS):
                if c != seen:
                    seen = c
                    pe.wait_ge(S[f"w_landed{c % 2}"], 16 * (c // 2 + 1))
                if n == 2:
                    pe.wait_ge(S["shn_ready"], 1)
                if n >= 3:
                    pe.wait_ge(S["proj_taken"], n - 2)
                for half in range(2):
                    for k in range(KT):
                        ins = mm(PS[0:width, 2 * (n % 3) + half, 0:HALF], wring[:, c % 2, k, c0:c0 + width],
                                 xnT[:, k, half * HALF:(half + 1) * HALF], start=(k == 0), stop=(k == KT - 1))
                ins.then_inc(S["proj_ready"], 1)
                if dest[0] == "f":
                    v_rows()
                    k_rows()
            pe.wait_ge(S["log_ready"], 1)
            o = nat_slot()
            for i in range(NTILE):
                tr(o[:, i * H:(i + 1) * H], LT[0:H, i * P:(i + 1) * P], ident[0:H, 0:H])
            tr(o[:, NTILE * H:(NTILE + 1) * H], f2[0:H, 0:P], ident[0:H, 0:H]).then_inc(S["nat_ready"], 1)

            pe.wait_ge(S["proj_taken"], len(ITEMS))
            for h in range(H):
                if h >= 3:
                    pe.wait_ge(S["ncb_taken"], h - 2)
                for half in range(2):
                    ins = mm(PS[:, 2 * (h % 3) + half, 0:NPT // 2], sel[0:H, h, :],
                             cT[0:H, 1 + half * (NPT // 2):1 + (half + 1) * (NPT // 2)], start=True, stop=True)
                ins.then_inc(S["ncb_ready"], 1)
            pe.wait_ge(S["ncb_taken"], H)
            pe.wait_ge(S["nat_taken"], 12)
            pe.wait_ge(S["pt_zero"], 1)

            def scores(n):
                g, i, hp = n // 8, n // 2 % 4, n % 2
                if n >= 2:
                    pe.wait_ge(S["s_added"], n - 1)
                nk = (NMETA + P * (i + 1)) // 2
                lo = 64 * hp
                for half in range(2):
                    ins = mm(PS[:, 2 * hp + half, 0:nk], qT[lo:lo + 64, g, 17 + P * i:17 + P * (i + 1)],
                             kT[lo:lo + 64, g, 1 + half * nk:1 + (half + 1) * nk], start=True, stop=True)
                ins.then_inc(S["s_ready"], 1)

            def turn_probs(n):
                i = n // 2 % 4
                pe.wait_ge(S["p_ready"], n + 1)
                if n >= 1:
                    pe.wait_ge(S["pt_taken"], n)
                tr(PS[0:NMETA, 5, 0:P], Sp[:, n % 3, 0:NMETA], ident)
                for kt in range(i + 1):
                    ins = tr(PS[:, 4, kt * P:(kt + 1) * P], Sp[:, n % 3, NMETA + kt * P:NMETA + (kt + 1) * P], ident)
                ins.then_inc(S["pt_ready"], 1)

            def weigh_values(n):
                g, i, hp = n // 8, n // 2 % 4, n % 2
                it = n // 2
                pe.wait_ge(S["pt_taken"], n + 1)
                if it >= 2 and hp == 0:
                    pe.wait_ge(S["o_taken"], it - 1)
                vc = slice((2 * g + hp) * HD, (2 * g + hp + 1) * HD)
                o = PS[64 * hp:64 * hp + 64, 6 + it % 2, 0:P]
                for kt in range(i + 1):
                    mm(o, vnat[:, 1 + kt, vc], PT[:, n % 2, kt, :], start=(kt == 0), stop=False)
                mm(o, vnat[:, 0, vc], PT[:, n % 2, 4, :], start=False, stop=True).then_inc(S["pv_ready"], 1)

            for n in range(3):
                scores(n)
            for n in range(32):
                turn_probs(n)
                if n + 3 < 32:
                    scores(n + 3)
                if n >= 1:
                    weigh_values(n - 1)
            weigh_values(31)

            pe.wait_ge(S["o_taken"], 16)
            pe.wait_ge(S["lr_in"], 48)
            pe.wait_ge(S["lr_act"], 2)
            HT = TL // 2
            for j in range(12):
                g = j % 4
                if j >= 3:
                    pe.wait_ge(S["lr_taken"], j - 2)
                for half in range(2):
                    c = slice(half * HT, (half + 1) * HT)
                    o = PS[:, 2 * (j % 3) + half, 0:HT]
                    w = slice(g * P, (g + 1) * P)
                    if j < 4:
                        ins = mm(o, WA[0:64, w], XR[0:64, 12, c], start=True, stop=True)
                    elif j < 8:
                        ins = mm(o, WA[64:P, w], XR[64:P, 12, c], start=True, stop=True)
                    else:
                        ins = mm(o, G2[:, w], XR[:, 13, c], start=True, stop=True)
                ins.then_inc(S["lr_ready"], 1)
            pe.wait_ge(S["lr_taken"], 12)

            def row_sums_of(src, step):
                pe.wait_ge(S["hs_in"], step)
                for half in range(2):
                    for g in range(NG):
                        ins = mm(PS[32 * g:32 * g + 32, half, 0:HT], headones[:, 48:80], src[:, g, half * HT:(half + 1) * HT],
                                 start=True, stop=True, skip_group_check=True)
                ins.then_inc(S["hs_rows"], 1)

            def head_sums(src, turn, step):
                pe.wait_ge(S["hs_in"], step)
                for g in range(NG):
                    n = 4 * (turn - 1) + g
                    if n >= 3:
                        pe.wait_ge(S["hs_taken"], n - 2)
                    for half in range(2):
                        c, rows = slice(half * HT, (half + 1) * HT), slice(32 * g, 32 * g + 32)
                        o = PS[:, 2 * (n % 3) + half, 0:HT]
                        if src is Rn:
                            ins = mm(o, spread[rows], Rn[rows, c], start=True, stop=True)
                        else:
                            ins = mm(o, headones, src[:, g, c], start=True, stop=True)
                    ins.then_inc(S["hs_ready"], 1)

            row_sums_of(T2, 1)
            head_sums(Rn, 1, 2)
            head_sums(T2, 2, 3)
            pe.wait_ge(S["hs_taken"], 8)
            pe.wait_ge(S["pre_done"], 1)

            for t in range(NTILE):
                c0 = t * P
                tile = slice(c0, c0 + P)
                nlev = 3 if t == 0 else 5
                lev0 = 0 if t == 0 else 3 + 5 * (t - 1)
                ch0 = 0 if t == 0 else 1 + 2 * (t - 1)
                for w, src in enumerate((AR[:, 0], Bd, Kd, XR[:, 8:12, :])):
                    if t:
                        pe.wait_ge(S["y_taken"], t)
                        pe.wait_ge(S["prev_tile"], t)
                    for g in range(NG):
                        ins = tr(PS[:, w, g * P:(g + 1) * P], src[:, g, tile], ident)
                    ins.then_inc(S["turned"], 1)
                for q in range(H):
                    g, lo = q % 4, 64 * (q // 4)
                    ins = mm(PS[:, 4 + q // 2, (q % 2) * 256:(q % 2) * 256 + 256], Bd[lo:lo + 64, g, tile],
                             AR[lo:lo + 64, :, g, tile], start=True, stop=True)
                    if q % 2:
                        ins.then_inc(S["gram_b"], 1)
                for q in range(H):
                    g, lo = q % 4, 64 * (q // 4)
                    if q % 4 == 0:
                        pe.wait_ge(S["turned_taken"], 4 * t + 1 + q // 4)
                    ins = mm(PS[:, q // 4, g * P:(g + 1) * P], AR[lo:lo + 64, 0, g, tile], Bd[lo:lo + 64, g, tile],
                             start=True, stop=True)
                    if q % 4 == 3:
                        ins.then_inc(S["gram_m"], 1)
                for q in range(H):
                    g, lo = q % 4, 64 * (q // 4)
                    if q % 2 == 0:
                        pe.wait_ge(S["gram_b_taken"], 4 * t + q // 2 + 1)
                    ins = mm(PS[:, 4 + q // 2, (q % 2) * 256:(q % 2) * 256 + 256], Kd[lo:lo + 64, g, tile],
                             AR[lo:lo + 64, :, g, tile], start=True, stop=True)
                    if q % 2:
                        ins.then_inc(S["gram_k"], 1)

                def turn_g(n, grp):
                    pe.wait_ge(S["turned_taken"], 4 * t + 4)
                    if n:
                        pe.wait_ge(S["x_taken"], 2 * (lev0 + (n - 1)) + grp + 1)
                    for i in range(4):
                        ins = tr(PS[:, 2 + grp, i * P:(i + 1) * P], MtRb[:, 4 * grp + i, 0, :], ident)
                    ins.then_inc(S["x_turned"], 1)

                pe.wait_ge(S["g_first"], t + 1)
                for grp in range(2):
                    turn_g(0, grp)
                pe.wait_ge(S["gram_k_taken"], 4 * t + 4)
                for l in range(nlev):
                    n = 2 * (lev0 + l)
                    for grp in range(2):
                        if l:
                            pe.wait_ge(S["g_added"], n + grp - 1)
                        for i in range(4):
                            q = 4 * grp + i
                            ins = mm(PS[:, 4 + grp, i * P:(i + 1) * P], Ms[:, q, :], MtRb[:, q, 0, :], start=True, stop=True)
                        ins.then_inc(S["r_ready"], 1)
                    for grp in range(2):
                        pe.wait_ge(S["r_taken"], n + grp + 1)
                        pe.wait_ge(S["x_taken"], n + grp + 1)
                        for i in range(4):
                            q = 4 * grp + i
                            ins = mm(PS[:, 6 + grp, i * P:(i + 1) * P], Xs[:, q, :], Rs[:, q, :], start=True, stop=True)
                        ins.then_inc(S["g_ready"], 1)
                    if l < nlev - 1:
                        for grp in range(2):
                            pe.wait_ge(S["g_added"], n + grp + 1)
                            turn_g(l + 1, grp)
                pe.wait_ge(S["g_added"], 2 * (lev0 + nlev))
                A_, B_, K_, V_ = range(4)
                for h in range(H):
                    q = 4 * (h % 2) + h // 2
                    hc = slice(h * HD, (h + 1) * HD)
                    ins = mm(PS[:, 0, hc], NtRk[:, q, 0, :], nat_[:, V_, hc], start=(h == 0), stop=(h == H - 1),
                             skip_group_check=True)
                ins.then_inc(S["nv_ready"], 1)
                for h in range(H):
                    g, hp = h // 2, h % 2
                    q, hc = 4 * hp + g, slice(h * HD, (h + 1) * HD)
                    ins = mm(PS[64 * hp:64 * hp + 64, 1, g * P:(g + 1) * P], nat_[:, A_, hc], MtRb[:, q, 0, :],
                             start=(g == 0), stop=(g == 3), skip_group_check=True)
                ins.then_inc(S["wt_ready"], 1)
                if t == 2:
                    pe.wait_ge(S["tot_ready"], 1)
                    totals = Rt[:, :, :, PAGE - 1:PAGE].rearrange("p t h o -> p (t h o)")
                    mm(PS[:, 7, 0:2 * H], later_page, totals, start=True, stop=False)
                    mm(PS[:, 7, 0:2 * H], ident, totals, start=False, stop=True).then_inc(S["later_sum"], 1)
                for h in range(H):
                    g, hp = h // 2, h % 2
                    q, hc = 4 * hp + g, slice(h * HD, (h + 1) * HD)
                    mm(PS[64 * hp:64 * hp + 64, 3, g * P:(g + 1) * P], nat_[:, V_, hc], NtRk[:, q, 1, :],
                       start=(g == 0), stop=False, skip_group_check=True)
                pe.wait_ge(S["nv_taken"], t + 1)
                for h in range(H):
                    q, hc = 4 * (h % 2) + h // 2, slice(h * HD, (h + 1) * HD)
                    mm(PS[:, 2, hc], MtRb[:, q, 0, :], NVs[:, hc], start=(h == 0), stop=False, skip_group_check=True)
                pe.wait_ge(S["wt_taken"], t + 1)
                for c in range(1 if t == 0 else 2):
                    r0, n = 64 * c, ch0 + c
                    rows = slice(r0, r0 + 64)
                    pe.wait_ge(S["st_done"], n + 1)
                    for g in range(NG):
                        ins = mm(PS[rows, 2, g * P:(g + 1) * P], Wt[:, g, rows], ST[:, g, :], start=False, stop=True,
                                 skip_group_check=True)
                    ins.then_inc(S["u_ready"], 1)
                    for g in range(NG):
                        mm(PS[:, 3, g * P + r0:g * P + r0 + 64], ST[:, g, :], AR[:, 1, g, c0 + r0:c0 + r0 + 64],
                           start=False, stop=False, skip_group_check=True)
                    for w in (K_, B_):
                        if w == B_:
                            pe.wait_ge(S["u_taken"], n + 1)
                        for h in range(H):
                            g, hp, hc = h // 2, h % 2, slice(h * HD, (h + 1) * HD)
                            src = nat_[rows, V_, hc] if w == K_ else Us[rows, hc]
                            ins = mm(PS[64 * hp:64 * hp + 64, 4, g * HD:(g + 1) * HD], nat_[rows, w, hc], src,
                                     start=(w == K_ and g == 0), stop=(w == B_), skip_group_check=True)
                    ins.then_inc(S["st_ready"], 1)
                if t == 0:
                    pe.wait_ge(S["s0_in0"], 128)
                    for b in range(DB):
                        if b == DB // 2:
                            pe.wait_ge(S["s0_in1"], 128)
                        if b >= 2:
                            pe.wait_ge(S["s0_taken"], b - 1)
                        for g in range(NG):
                            ins = tr(PS[:, 6 + b % 2, g * P:(g + 1) * P], S0n[:, b % (DB // 2), g, :], ident)
                        ins.then_inc(S["s0_turned"], 1)
                    pe.wait_ge(S["s0_taken"], DB)
                    for b in range(DB):
                        tok = slice(64 + DS * b, 64 + DS * (b + 1))
                        for g in range(NG):
                            mm(PS[:, 5, g * NS + DS * b:g * NS + DS * (b + 1)], S0T[:, b, g, :], Wt[:, g, tok],
                               start=(b == 0 and g == 0), stop=True, skip_group_check=True)
                            ins = mm(PS[:, 3, g * P + tok.start:g * P + tok.stop], S0T[:, b, g, :], AR[:, 1, g, tok],
                                     start=False, stop=False, skip_group_check=True)
                    ins.then_inc(S["ut_ready"], 1)
                    pe.wait_ge(S["ut_taken"], 1)
                    for g in range(NG):
                        ins = mm(PS[64:P, 2, g * P:(g + 1) * P], UTs[:, g, :], ident, start=False, stop=True,
                                 skip_group_check=True)
                    ins.then_inc(S["us_ready"], 1)
                    pe.wait_ge(S["us_taken"], 1)
                else:
                    pe.wait_ge(S["u_taken"], ch0 + 2)
                for h in range(H):
                    g, hp = h // 2, h % 2
                    q, hc = 4 * hp + g, slice(h * HD, (h + 1) * HD)
                    ins = mm(PS[64 * hp:64 * hp + 64, 3, g * P:(g + 1) * P], Us[:, hc], MtRb[:, q, 1, :],
                             start=False, stop=(g == 3), skip_group_check=True)
                ins.then_inc(S["y_ready"], 1)
                if t == 0:
                    for g in range(NG):
                        for hp in range(2):
                            h = 2 * g + hp
                            hc = slice(h * HD, (h + 1) * HD)
                            pe.wait_ge(S["um_ready"], h + 1)
                            o = PS[64 * hp:64 * hp + 64, 6 + g % 2, :]
                            if g >= 2 and hp == 0:
                                pe.wait_ge(S["sn_taken"], g - 1)
                            mm(o, nat_[64:P, K_, hc], Um[64:P, 1].rearrange("p b i -> p (b i)"), start=True, stop=False)
                            ins = mm(o, nat_[64:P, B_, hc], Um[64:P, 0].rearrange("p b i -> p (b i)"), start=False, stop=True)
                            ins.then_inc(S["sn_ready"], 1)
                    for g in range(NG):
                        pe.wait_ge(S["sn_taken"], g + 1)
                        if g:
                            pe.wait_ge(S["so_taken"], g)
                        for b in range(DB):
                            ins = tr(PS[0:64, b // 4, (b % 4) * P:(b % 4 + 1) * P], Sn[:, g, b * HD:(b + 1) * HD], ident)
                        ins.then_inc(S["so_turned"], 1)
                    pe.wait_ge(S["so_taken"], NG)
            pe.wait_ge(S["st_done"], 10)
            pe.wait_ge(S["y_taken"], NTILE)
            for g in range(NG):
                ins = tr(PS[:, 0, g * P:(g + 1) * P], ST[:, g, :], ident)
            ins.then_inc(S["fs_turned"], 1)
            pe.wait_ge(S["fs_taken"], 1)
            head_sums(YT, 3, 4)
            pe.wait_ge(S["hs_taken"], 12)
            row_sums_of(T2, 5)
            head_sums(Rn, 4, 6)
            pe.wait_ge(S["hs_taken"], 16)
            pe.wait_ge(S["rwkv_done"], 1)
            pe.wait_ge(S["rn_padded"], 1)
            for b in range(DB):
                ins = tr(PS[:, 2 + b // 4, (b % 4) * P:(b % 4 + 1) * P], RNp[:, b].rearrange("p a b -> p (a b)"), ident)
            ins.then_inc(S["rn_turned"], 1)

            def turn_keys(b, p):
                if p % LOT == 0:
                    pe.wait_ge(k_in[p % NRING // LOT], LOT * (32 * b + 16 * (p // NRING + 1)))
                if p >= 2 or not (isinstance(b, int) and b == 0):
                    pe.wait_ge(S["kt_taken"], b * NPG + (p - 1))
                for g in range(NG):
                    ins = tr(PS[:, p % 2, g * P:(g + 1) * P], Kr[:, p % NRING, g * P:(g + 1) * P], ident)
                ins.then_inc(S["k_free"], 1)

            def page_scores(b, p):
                j = p // LOT
                pe.wait_ge(S["kt_taken"], b * NPG + (p + 1))
                if p == 0:
                    pe.wait_ge(S["qc_ready"], b + 1)
                    if isinstance(b, int):
                        pe.wait_ge(S["rn_taken"], 1)
                if p % LOT == 0 and (j >= 2 or not (isinstance(b, int) and b == 0)):
                    pe.wait_ge(S["sc_taken"], b * NLOT + (j - 1))
                for g in range(NG):
                    ins = mm(PS[ROWS[g], 2 + j % 2, (p % LOT) * P:(p % LOT + 1) * P], Qc[:, g, :], KTs[:, p % 2, g, :],
                             start=True, stop=True, skip_group_check=True)
                ins.then_inc(S["sc_page"], 1)

            def new_scores(b):
                if not isinstance(b, int):
                    pe.wait_ge(S["prn_taken"], b)
                for g in range(NG):
                    ins = mm(PS[ROWS[g], 7, 0:P], Qc[:, g, :], kTS[:, g, :], start=True, stop=True, skip_group_check=True)
                ins.then_inc(S["new_ready"], 1)

            def turn_new(b):
                pe.wait_ge(S["exp_out"], b * NEXP + 1)
                tr(PS[:, 7, P:2 * P], Pb[:, 0, :], ident).then_inc(S["prn_turned"], 1)

            def turn_probs(b, j):
                pe.wait_ge(S["exp_out"], b * NEXP + (LOT * (j + 1) // 11 + 1))
                if j >= 2:
                    pe.wait_ge(S["pr_taken"], b * NLOT + (j - 1))
                for i in range(LOT):
                    ins = tr(PS[:, 5 + j % 2, i * P:(i + 1) * P], Pb[:, 1 + LOT * j + i, :], ident)
                ins.then_inc(S["pr_turned"], 1)

            def new_values(b):
                pe.wait_ge(S["prn_taken"], b + 1)
                for g in range(NG):
                    mm(PS[ROWS[g], 4, 0:P], PTn[:, ROWS[g]], vnat[:, 0, g * P:(g + 1) * P],
                       start=True, stop=False, skip_group_check=True)

            def lot_values(b, j):
                pe.wait_ge(v_in[j % (NRING // LOT)], LOT * (32 * b + 16 * (j // (NRING // LOT) + 1)))
                pe.wait_ge(S["pr_taken"], b * NLOT + (j + 1))
                for p in range(LOT * j, LOT * (j + 1)):
                    for g in range(NG):
                        ins = mm(PS[ROWS[g], 4, 0:P], PTs[:, j % 2, p % LOT, ROWS[g]], Vr[:, p % NRING, g * P:(g + 1) * P],
                                 start=False, stop=(p == NPG - 1), skip_group_check=True)
                    ins.then_inc(S["v_free"], 1)

            def turn_output(b):
                pe.wait_ge(S["o_scaled"], b + 1)
                tr(PS[:, 4, P:2 * P], Oc, ident).then_inc(S["o_turned"], 1)

            def pass_pages(b, prev):
                for j in range(NLOT):
                    for p in range(LOT * j, LOT * (j + 1)):
                        turn_keys(b, p)
                        if p:
                            page_scores(b, p - 1)
                    if prev:
                        if j == 0:
                            turn_new(b - 1)
                        turn_probs(b - 1, j)
                        if j == 1:
                            new_values(b - 1)
                    if j == 1:
                        new_scores(b)
                    if prev:
                        if j >= 1:
                            lot_values(b - 1, j - 1)
                page_scores(b, NPG - 1)
                if prev:
                    lot_values(b - 1, NLOT - 1)
                    turn_output(b - 1)

            pass_pages(0, False)
            with pe.Fori(1, DB) as b:
                pass_pages(b, True)

            def rows_of(i):
                return (slice(64, P), slice(SEQ, OUTC)) if i == 0 else (slice(0, P), slice((i - 1) * P, i * P))

            order = [1, 2, 3, 4, 0]

            def project(n):
                rows, cols = rows_of(order[n])
                if n >= 2:
                    pe.wait_ge(S["h_ready"], n - 1)
                for half in range(2):
                    for k in range(KT):
                        ins = mm(PS[rows, 2 * (n % 2) + half, :], mixT[:, k, cols], wo[:, k, half * NB:(half + 1) * NB],
                                 start=(k == 0), stop=(k == KT - 1))
                ins.then_inc(S["mixed_out"], 1)

            turn_new(DB - 1)
            pe.wait_ge(S["sc_taken"], DB * NLOT)
            for j in range(NLOT):
                if j == 0:
                    pe.wait_ge(S["wo_in"], 16)
                if j % 2 == 0:
                    project(j // 2)
                turn_probs(DB - 1, j)
                if j == 0:
                    new_values(DB - 1)
                else:
                    lot_values(DB - 1, j - 1)
            lot_values(DB - 1, NLOT - 1)
            turn_output(DB - 1)

            pe.wait_ge(S["attn_done"], 1)

            def turn_h(n):
                rows, cols = rows_of(order[n])
                w = cols.stop - cols.start
                pe.wait_ge(S["xs_ready"], NTILE + n + 1)
                if n >= 2:
                    pe.wait_ge(S["xnT_ready"], NTILE + n - 1)
                for f in range(KT):
                    ins = tr(PS[:, 4 + 2 * (n % 2) + f // 4, (f % 4) * w:(f % 4 + 1) * w], xs2[rows, n % 2, f * P:(f + 1) * P],
                             ident[rows, rows])
                ins.then_inc(S["xT_turned"], 1)

            turn_h(0)
            turn_h(1)
            project(4)
            for n in range(2, NTILE):
                turn_h(n)
            pe.wait_ge(S["xnT_ready"], 2 * NTILE)
            HO = OUTC // 2
            for f in range(NF):
                r = f // 2
                if f % 2 == 0:
                    pe.wait_ge(f_in[r % FR], 32 * (r // FR + 1))
                if f >= 2:
                    pe.wait_ge(S["act_ready"], f - 1)
                for w in range(2):
                    for half in range(2):
                        for k in range(KT):
                            c = w * 2048 + k * 256 + (f % 2) * P
                            ins = mm(PS[:, 4 * (f % 2) + 2 * w + half, 0:HO], fring[:, (r + 2) % FR, c:c + P],
                                     hT[:, k, half * HO:(half + 1) * HO], start=(k == 0), stop=(k == KT - 1))
                ins.then_inc(S["gu_ready"], 1)
            pe.wait_ge(S["act_ready"], NF)
            for half in range(2):
                for c in range(3):
                    r = 11 + 3 * half + c
                    pe.wait_ge(f_in[r % FR], 32 * (r // FR + 1))
                    ks = range(8 * c, min(8 * c + 8, NF))
                    pairs = [(k, n) for k in ks for n in range(NTILE)] if c < 2 else [(k, n) for n in range(NTILE) for k in ks]
                    for k, n in pairs:
                        rows, cols = rows_of(order[n])
                        if half and k == 0 and n >= 3:
                            pe.wait_ge(S["down_taken"], n - 2)
                        ins = mm(PS[rows, (5 * half + n) % 8, :], actT[:, k, cols],
                                 fring[:, (r + 2) % FR, (k - 8 * c) * NB:(k - 8 * c + 1) * NB], start=(k == 0), stop=(k == NF - 1))
                        if k == NF - 1 and n < NTILE - 1:
                            ins.then_inc(S["down_tile"], 1)
                    ins.then_inc(S["down_used"], 1)

        @block.scalar
        def _(act):
            ch = Chain(act, S["act_c"])
            av = nc.scalar.activation
            act.wait_ge(S["par_turned"], 1)
            av(par[:, 0:NPAR], PS[:, 7, 0:NPAR], ACT.Copy).then_inc(S["par_ready"], 1)
            for i in range(NTILE):
                act.wait_ge(x_in[i], 48 if i == 0 else 16)
                if i == 0:
                    act.wait_ge(S["consts"], 1)
                ch(av(xsq, x[:, i, :], ACT.Square, accum_out=ss[:, i:i + 1]))
                ch.wait()
                nc.scalar.activation(rstd[:, i:i + 1], ss[:, i:i + 1], ACT.Copy).then_inc(S["square_done"], 1)
                act.wait_ge(S["var_done"], i + 1)
                av(ss[:, i:i + 1], rstd[:, i:i + 1], ACT.Sqrt).then_inc(S["std_done"], 1)
            act.wait_ge(S["shn_turned"], 1)
            av(shn[0:9, :].rearrange("p (a b) -> p a b", a=2), PS[0:9, 4:6, :], ACT.Copy).then_inc(S["shn_ready"], 1)
            for n, (c, c0, width, dest) in enumerate(ITEMS):
                act.wait_ge(S["proj_ready"], n + 1)
                src = PS[0:width, 2 * (n % 3):2 * (n % 3) + 2, 0:HALF]
                kind, g = dest
                if kind == "rw":
                    if g >= 2:
                        act.wait_ge(S["mixed_done"], g - 1)
                    dst, scale = raw[:, g % 2, :], 1.0
                elif kind == "f":
                    dst, scale = fT[0:H], 1.0
                else:
                    dst, scale = (qT if kind == "q" else kT)[:, g, :], (HD ** -0.5 if kind == "q" else 1.0)
                av(dst.rearrange("p (a b) -> p a b", a=2), src, ACT.Copy, scale=scale).then_inc(S["proj_taken"], 1)
                if kind == "f":
                    act.wait_ge(S["f_in"], 16)
                    act.wait_ge(S["proj_taken"], n + 1)
                    ch(av(cT[0:H], fT[0:H], ACT.Abs, bias=bf_col[0:H]))
                    ch.wait()
                    ch(av(cT[0:H], cT[0:H], ACT.Exp, scale=-1.0))
                    ch.wait()
                    av(f2[0:H], cT[0:H], ACT.Ln, bias=1.0).then_inc(S["logf_a"], 1)
            for h in range(H):
                act.wait_ge(S["ncb_ready"], h + 1)
                av(NCB[:, h, :].rearrange("p (a b) -> p a b", a=2), PS[:, 2 * (h % 3):2 * (h % 3) + 2, 0:NPT // 2],
                   ACT.Copy, scale=-1.0).then_inc(S["ncb_taken"], 1)

            def take_pt(n):
                i = n // 2 % 4
                act.wait_ge(S["pt_ready"], n + 1)
                if n >= 2:
                    act.wait_ge(S["pv_ready"], n - 1)
                av(PT[:, n % 2, 0:i + 1, :], PS[:, 4, 0:(i + 1) * P].rearrange("p (a b) -> p a b", b=P), ACT.Copy)
                av(PT[0:NMETA, n % 2, 4, :], PS[0:NMETA, 5, 0:P], ACT.Copy).then_inc(S["pt_taken"], 1)

            def take_o(it):
                act.wait_ge(S["pv_ready"], 2 * it + 2)
                g, i = it // 4, it % 4
                av(mixT[:, g, i * P:(i + 1) * P], PS[:, 6 + it % 2, 0:P], ACT.Copy).then_inc(S["o_taken"], 1)

            for n in range(32):
                i = n // 2 % 4
                act.wait_ge(S["mx_ready"], n + 1)
                sv = Sp[:, n % 3, 0:NMETA + P * (i + 1)]
                av(sv, sv, ACT.Exp, bias=nmp[:, n % 3:n % 3 + 1], accum_out=smp[:, n % 3:n % 3 + 1]).then_inc(S["exp_done"], 1)
                if n >= 1:
                    take_pt(n - 1)
                if n >= 2 and n % 2 == 0:
                    take_o((n - 2) // 2)
            take_pt(31)
            take_o(15)

            ch.wait()
            act.wait_ge(S["mixed_done"], 14)
            av(XR[0:64, 12, :], XR[0:64, 12, :], ACT.Tanh).then_inc(S["lr_act"], 1)
            av(XR[:, 13, :], XR[:, 13, :], ACT.Sigmoid).then_inc(S["lr_act"], 1)
            act.wait_ge(S["pv_ready"], 32)
            for j in range(12):
                g = j % 4
                act.wait_ge(S["lr_ready"], j + 1)
                src = PS[:, 2 * (j % 3):2 * (j % 3) + 2, 0:TL // 2]
                dst = (AR[:, 0, g] if j < 4 else Bd[:, g] if j < 8 else gate[:, g]).rearrange("p (a b) -> p a b", a=2)
                if j < 8:
                    av(dst, src, ACT.Sigmoid, bias=pc("w0" if j < 4 else "a0", g)).then_inc(S["lr_taken"], 1)
                else:
                    av(dst, src, ACT.Copy).then_inc(S["lr_taken"], 1)
            act.wait_ge(S["L_ready"], 1)
            av(AR[:, 1], Kd, ACT.Exp).then_inc(S["decays"], 1)
            av(AR[:, 0], AR[:, 0], ACT.Exp).then_inc(S["decays"], 1)
            act.wait_ge(S["decays"], 1)
            av(Kd, Kd, ACT.Exp, scale=-1.0).then_inc(S["decays"], 1)
            act.wait_ge(S["root_in"], 1)
            av(Rn, Rn, ACT.Sqrt).then_inc(S["root_done"], 1)

            act.wait_ge(S["pre_done"], 1)
            for t in range(NTILE):
                nlev = 3 if t == 0 else 5
                lev0 = 0 if t == 0 else 3 + 5 * (t - 1)
                if t:
                    act.wait_ge(S["y_ready"], t)
                    act.wait_ge(S["st_ready"], 1 + 2 * (t - 1))
                    if t == 1:
                        act.wait_ge(S["sn_ready"], H)
                for w in range(4):
                    act.wait_ge(S["turned"], 4 * t + w + 1)
                    av(nat_[:, w, :], PS[:, w, :], ACT.Copy).then_inc(S["turned_taken"], 1)
                for l in range(nlev):
                    for grp in range(2):
                        n = 2 * (lev0 + l) + grp
                        act.wait_ge(S["x_turned"], n + 1)
                        if l:
                            act.wait_ge(S["g_ready"], n - 1)
                        av(Xs[:, 4 * grp:4 * grp + 4, :], PS[:, 2 + grp, :].rearrange("p (a b) -> p a b", a=4),
                           ACT.Copy).then_inc(S["x_taken"], 1)
                act.wait_ge(S["nv_ready"], t + 1)
                av(NVs, PS[:, 0, :], ACT.Copy).then_inc(S["nv_taken"], 1)
                act.wait_ge(S["wt_ready"], t + 1)
                av(Wt, PS[:, 1, :].rearrange("p (a b) -> p a b", a=NG), ACT.Copy).then_inc(S["wt_taken"], 1)
                if t == 0:
                    for b in range(DB):
                        act.wait_ge(S["s0_turned"], b + 1)
                        av(S0T[:, b], PS[:, 6 + b % 2, :].rearrange("p (a b) -> p a b", a=NG), ACT.Copy).then_inc(S["s0_taken"], 1)
                    act.wait_ge(S["ut_ready"], 1)
                    av(UTs, PS[:, 5, 0:NG * NS].rearrange("p (a b) -> p a b", a=NG), ACT.Copy).then_inc(S["ut_taken"], 1)
                act.wait_ge(S["y_ready"], t + 1)
                av(YT[:, :, t * P:(t + 1) * P], PS[:, 3, :].rearrange("p (a b) -> p a b", a=NG), ACT.Copy).then_inc(S["y_taken"], 1)
                if t == 0:
                    for g in range(NG):
                        act.wait_ge(S["so_turned"], g + 1)
                        if g >= 2:
                            act.wait_ge(S[f"so_out{g % 2}"], 32)
                        av(SOo[0:64, g % 2], PS[0:64, 0:2, :].rearrange("p a (b c) -> p (a b) c", b=4), ACT.Copy)\
                            .then_inc(S["so_taken"], 1)
            act.wait_ge(S["fs_turned"], 1)
            av(Xs[:, 0:NG, :], PS[:, 0, :].rearrange("p (a b) -> p a b", a=NG), ACT.Copy).then_inc(S["fs_taken"], 1)
            act.wait_ge(S["yc_ready"], 1)
            act.wait_ge(S["fs_out"], 32)
            av(T2, YT, ACT.Square).then_inc(S["hs_in"], 1)
            act.wait_ge(S["root_in"], 2)
            av(Rn, Rn, ACT.Sqrt).then_inc(S["root_done"], 1)

            act.wait_ge(S["rn_turned"], 1)
            av(RNT, PS[:, 2:4, :].rearrange("p a (b n) -> p (a b) n", n=P), ACT.Copy).then_inc(S["rn_taken"], 1)

            def take_keys(b, p):
                act.wait_ge(S["k_free"], b * NPG + (NRING + p + 1))
                if p >= 2 or not (isinstance(b, int) and b == 0):
                    act.wait_ge(S["sc_page"], b * NPG + (p - 1))
                av(KTs[:, p % 2], PS[:, p % 2, :].rearrange("p (g n) -> p g n", g=NG), ACT.Copy).then_inc(S["kt_taken"], 1)

            def exps(b, third):
                if third == 0:
                    act.wait_ge(S["max_steps"], 2 * b + 2)
                n = (NPG + 1) // NEXP
                av(Pb[:, third * n:(third + 1) * n, :], Sb[:, third * n:(third + 1) * n, :], ACT.Exp, bias=nm,
                   accum_out=ss3[:, third:third + 1]).then_inc(S["exp_out"], 1)

            for p in range(NPG):
                take_keys(0, p)
            with act.Fori(1, DB) as b:
                for p in range(NPG):
                    take_keys(b, p)
                    if p in (1, 3, 5):
                        exps(b - 1, p // 2)
            for third in range(NEXP):
                exps(DB - 1, third)

            def mean_of_squares(n, i, turn):
                rows = slice(64, P) if i == 0 else slice(0, P)
                act.wait_ge(S["h_ready"], turn * NTILE + n + 1)
                act.wait_ge(S["square_done"], (turn + 1) * NTILE + n)
                ch(av(xsq2[rows], x[rows, i, :], ACT.Square, accum_out=ss[rows, i:i + 1]))
                ch.wait()
                av(rstd[rows, i:i + 1], ss[rows, i:i + 1], ACT.Copy).then_inc(S["square_done"], 1)
                act.wait_ge(S["var_done"], (turn + 1) * NTILE + n + 1)
                av(ss[rows, i:i + 1], rstd[rows, i:i + 1], ACT.Sqrt).then_inc(S["std_done"], 1)

            for n, i in enumerate([1, 2, 3, 4, 0]):
                mean_of_squares(n, i, 0)
            HO = OUTC // 2
            for f in range(NF):
                act.wait_ge(S["gu_ready"], f + 1)
                if f >= 2:
                    act.wait_ge(S["act_ready"], f - 1)
                av(sgate[:, f % 2, :].rearrange("p (a b) -> p a b", a=2), PS[:, 4 * (f % 2):4 * (f % 2) + 2, 0:HO], ACT.Silu)\
                    .then_inc(S["silu_done"], 1)
            for n, i in enumerate([1, 2, 3, 4, 0]):
                mean_of_squares(n, i, 1)

        @block.vector
        def _(dve):
            ch = Chain(dve, S["dve_c"])
            v = nc.vector
            tt, ts, stt = v.tensor_tensor, v.tensor_scalar, v.scalar_tensor_tensor
            dve.wait_ge(S["consts"], 1)

            def mean_square(i):
                dve.wait_ge(S["square_done"], i + 1)
                ts(rstd[:, i:i + 1], rstd[:, i:i + 1], 1.0 / D, RMS_EPS, ALU.mult, ALU.add).then_inc(S["var_done"], 1)

            for i in range(NTILE):
                mean_square(i)
                dve.wait_ge(S["std_done"], i + 1)
                ch(v.reciprocal(rstd[:, i:i + 1], ss[:, i:i + 1]))
                ch.wait()
                if i == 0:
                    ch(v.memset(rstd[32:32 + DB, 0:1], 1.0))
                    ch.wait()
                if i >= 2:
                    dve.wait_ge(S["xT_turned"], i - 1)
                ts(xs[:, i % 2, :], x[:, i, :], rstd[:, i:i + 1], None, ALU.mult).then_inc(S["xs_ready"], 1)
                if i == 0:
                    dve.wait_ge(S["par_ready"], 1)
                dve.wait_ge(S["xT_turned"], i + 1)
                for hf in range(2):
                    gain = par[:, pcol["ln1_g"] + 4 * hf:pcol["ln1_g"] + 4 * hf + 4].unsqueeze(2)
                    src = PS[:, 2 * (i % 2) + hf, :].rearrange("p (f c) -> p f c", c=P)
                    dst = xnT[:, 4 * hf:4 * hf + 4, :]
                    if i:
                        ins = tt(dst[:, :, 17 + P * (i - 1):17 + P * i], src, gain.to_broadcast([P, 4, P]), ALU.mult)
                    else:
                        tt(dst[:, :, 1:1 + NMETA], src[:, :, 0:NMETA], gain.to_broadcast([P, 4, NMETA]), ALU.mult)
                        for k in range(4):
                            ts(samp(dst[:, k, :], 1), src[:, k, 64:P].rearrange("p (b t) -> p b t", t=DS),
                               pc("ln1_g", 4 * hf + k), None, ALU.mult)
                        ins = v.tensor_copy(dst[:, :, RS0:RS0 + 9 * DB:9], src[:, :, 32:32 + DB])
                if i == 0:
                    ch(ins)
                    ch.wait()
                    ins = v.tensor_copy(xnS.rearrange("p k (b t) -> p k b t", t=DS), samps(xnT))
                ins.then_inc(S["xnT_ready"], 1)

            def take_nat(j):
                dve.wait_ge(S["nat_ready"], j + 1)
                src = PS[:, 6 + j % 2, :]
                if j < NTILE:
                    if j == 0:
                        v.tensor_copy(vnat[0:NMETA, 0, :], src[0:NMETA])
                        ins = v.tensor_copy(vnat[64:P, 0, :], src[64:P])
                    else:
                        ins = v.tensor_copy(vnat[:, j, :], src)
                elif j < NTILE + 6:
                    n = (NMETA, P, P, P, P, NS)[j - NTILE]
                    ins = v.tensor_copy(kn[64:P, 0, :] if n == NS else kn[0:n, j - NTILE, :], src[0:n])
                else:
                    v.tensor_copy(cnat, src[:, NTILE * H:(NTILE + 1) * H])
                    ins = v.tensor_copy(lognat, src[:, 0:NTILE * H].rearrange("p (i h) -> p i h", h=H))
                ins.then_inc(S["nat_taken"], 1)

            dve.wait_ge(S["consts"], 2)
            dve.wait_ge(S["proj_taken"], 2 * NG)
            v.tensor_copy(kTS[:, :, 64:P].rearrange("p g (b t) -> p g b t", t=DS), samps(kT)).then_inc(S["kts_ready"], 1)
            for j in range(11):
                take_nat(j)
            dve.wait_ge(S["logf_a"], 1)
            dve.wait_ge(S["f_in"], 16)
            ch(ts(fT[0:H], fT[0:H], bf_col[0:H], 0.0, ALU.add, ALU.min))
            ch.wait()
            ch(tt(fT[0:H], fT[0:H], f2[0:H], ALU.subtract))
            ch.wait()
            ch(v.tensor_tensor_scan(cT[0:H], forget_mask[0:H], fT[0:H], 0.0, ALU.mult, ALU.add))
            ch.wait()
            v.tensor_copy(LT[0:H, 0:NMETA], fT[0:H, 1:1 + NMETA])
            v.tensor_copy(LT[0:H, 64:P].rearrange("p (b t) -> p b t", t=DS), samp(fT[0:H], 1))
            v.tensor_copy(LT[0:H, P:TL], fT[0:H, 17:17 + SEQ])
            v.memset(f2[0:H, 0:64], 0.0)
            v.tensor_copy(f2[0:H, 64:P].rearrange("p (b t) -> p b t", t=DS), samp(cT[0:H], 1)).then_inc(S["log_ready"], 1)

            for n in range(14):
                dve.wait_ge(S["proj_taken"], NRW0 + n + 1)
                r = raw[:, n % 2, :]
                if n:
                    dve.wait_ge(S["mixed_done"], n)
                ch(tt(diff[:, 0:RAW - 1], r[:, 0:RAW - 1], r[:, 1:RAW], ALU.subtract))
                ch.wait()
                mu = pc("mu_shift", n)
                stt(XR[:, n, 0:NMETA], diff[:, 0:NMETA], mu, r[:, 1:1 + NMETA], ALU.mult, ALU.add)
                stt(XR[:, n, 64:P].rearrange("p (b t) -> p b t", t=DS), samp(diff, 0), mu, samp(r, 1), ALU.mult, ALU.add)
                stt(XR[:, n, P:TL], diff[:, 16:16 + SEQ], mu, r[:, 17:17 + SEQ], ALU.mult, ALU.add).then_inc(S["mixed_done"], 1)
            take_nat(11)
            dve.wait_ge(S["nat_taken"], 12)
            ch(tt(RN[64:P], RN[64:P], cnat[64:P].unsqueeze(1).unsqueeze(3).to_broadcast([64, DB, H, DS]), ALU.subtract))
            for hp in range(2):
                for g in range(NG):
                    ins = v.tensor_copy(QB[64 * hp:64 * hp + 64, :, g, 8 * hp:8 * hp + 8], samp(qT[64 * hp:64 * hp + 64, g, :], 1))
            ins.then_inc(S["qb_ready"], 1)
            dve.wait_ge(S["proj_ready"], len(ITEMS))
            v.memset(PT[:, :, 4, :], 0.0).then_inc(S["pt_zero"], 1)

            dve.wait_ge(S["ncb_taken"], H)
            for n in range(33):
                if n < 32:
                    g, i, hp = n // 8, n // 2 % 4, n % 2
                    nk = NMETA + P * (i + 1)
                    sv = Sp[:, n % 3, 0:nk]
                    dve.wait_ge(S["s_ready"], n + 1)
                    if n >= 3:
                        dve.wait_ge(S["pt_ready"], n - 2)
                    tt(sv.rearrange("p (a b) -> p a b", a=2), PS[:, 2 * hp:2 * hp + 2, 0:nk // 2],
                       NCB[:, 2 * g + hp, 0:nk].rearrange("p (a b) -> p a b", a=2), ALU.add).then_inc(S["s_added"], 1)
                    dve.wait_ge(S["s_added"], n + 1)
                    ch(tt(sv[:, nk - P:nk], sv[:, nk - P:nk], causal, ALU.add))
                    ch.wait()
                    ch(v.tensor_reduce(mxp[:, n % 3:n % 3 + 1], sv, AX.X, ALU.max))
                    ch.wait()
                    ts(nmp[:, n % 3:n % 3 + 1], mxp[:, n % 3:n % 3 + 1], -1.0, None, ALU.mult).then_inc(S["mx_ready"], 1)
                if n >= 1:
                    m = n - 1
                    if m >= 2:
                        dve.wait_ge(S["p_ready"], m)
                    dve.wait_ge(S["exp_done"], m + 1)
                    nk = NMETA + P * (m // 2 % 4 + 1)
                    ch(v.reciprocal(rcp[:, m % 3:m % 3 + 1], smp[:, m % 3:m % 3 + 1]))
                    ch.wait()
                    sv = Sp[:, m % 3, 0:nk]
                    ts(sv, sv, rcp[:, m % 3:m % 3 + 1], None, ALU.mult).then_inc(S["p_ready"], 1)

            HT = TL // 2

            def two(w):
                return w.rearrange("p (a b) -> p a b", a=2)

            def hs(n):
                return PS[:, 2 * (n % 3):2 * (n % 3) + 2, 0:HT]

            dve.wait_ge(S["lr_taken"], 8)
            ch(ts(AR[:, 0], AR[:, 0], -E_HALF, None, ALU.mult))
            ch.wait()
            for g in range(NG):
                ch(v.tensor_tensor_scan(Kd[:, g], chunk_mask, AR[:, 0, g], 0.0, ALU.mult, ALU.add))
            ch.wait()
            tt(AR[:, 0], Kd, AR[:, 0], ALU.subtract).then_inc(S["L_ready"], 1)
            dve.wait_ge(S["out_done"], 16 * N_FIRST_OUT)
            for g in range(NG):
                ch(ts(kk[:, g], XR[:, 4 + g], pc("k_k", g), None, ALU.mult))
            ch.wait()
            tt(T2, kk, kk, ALU.mult).then_inc(S["hs_in"], 1)
            dve.wait_ge(S["hs_rows"], 1)
            ts(two(Rn), PS[:, 0:2, 0:HT], 1e-24, None, ALU.max).then_inc(S["root_in"], 1)
            dve.wait_ge(S["root_done"], 1)
            v.reciprocal(Rn, Rn).then_inc(S["hs_in"], 1)
            for g in range(NG):
                dve.wait_ge(S["hs_ready"], g + 1)
                tt(two(kk[:, g]), hs(g), two(kk[:, g]), ALU.mult).then_inc(S["hs_taken"], 1)
            dve.wait_ge(S["hs_taken"], 4)
            for g in range(NG):
                ch(ts(T2[:, g], Bd[:, g], -1.0, pc("k_a", g), ALU.add, ALU.mult))
            ch.wait()
            ch(stt(XR[:, 4:8], T2, 1.0, XR[:, 4:8], ALU.add, ALU.mult))
            ch.wait()
            for g in range(NG):
                ins = stt(T2[:, g], XR[:, g], pc("r_k", g), XR[:, 4 + g], ALU.mult, ALU.mult)
            ins.then_inc(S["hs_in"], 1)
            dve.wait_ge(S["decays"], 3)
            ch(tt(Bd, Bd, kk, ALU.mult))
            ch(stt(AR[:, 0], kk, -1.0, AR[:, 0], ALU.mult, ALU.mult))
            ch(v.tensor_copy(Dc[:, :, 0:1], AR[:, 1, :, NMETA - 1:NMETA]))
            ch(v.tensor_copy(Dc[:, :, 1:1 + DB], AR[:, 1, :, 64 + DS - 1:P:DS]))
            ch(v.tensor_copy(Dc[:, :, 1 + DB:], AR[:, 1, :, P + 63:TL:64]))
            ch.wait()
            ch(tt(Bd, Bd, Kd, ALU.mult))
            ch(tt(AR[:, 1], XR[:, 0:4], AR[:, 1], ALU.mult))
            ch.wait()
            ch(tt(Kd, XR[:, 4:8], Kd, ALU.mult))
            for g in range(NG):
                dve.wait_ge(S["hs_ready"], NG + g + 1)
                tt(two(kk[:, g]), hs(NG + g), two(XR[:, 8 + g]), ALU.mult).then_inc(S["hs_taken"], 1)
            ch.wait()
            dve.wait_ge(S["hs_taken"], 2 * NG)
            ch(v.memset(S0n, 0.0))
            ch(v.memset(ST, 0.0))
            ch.wait()
            v.memset(Us, 0.0).then_inc(S["pre_done"], 1)
            dve.wait_ge(S["pre_done"], 1)
            v.memset(small[:, 1:2], 0.0).then_inc(S["st_done"], 1)

            for t in range(NTILE):
                nlev = 3 if t == 0 else 5
                lev0 = 0 if t == 0 else 3 + 5 * (t - 1)
                ch0 = 0 if t == 0 else 1 + 2 * (t - 1)
                kind = 0 if t == 0 else 1

                def masked(dst, src, mask, k):
                    return tt(dst, src, mask.unsqueeze(1).to_broadcast([P, k, P]), ALU.mult)

                if t == 0:
                    dve.wait_ge(S["lr_ready"], 12)
                else:
                    dve.wait_ge(S["y_ready"], t)
                if t == 1:
                    dve.wait_ge(S["so_out0"], 64)
                    dve.wait_ge(S["so_out1"], 64)
                    dve.wait_ge(S["um_used"], H)
                for j in range(4):
                    dve.wait_ge(S["gram_b"], 4 * t + j + 1)
                    src = PS[:, 4 + j, :].rearrange("p (q w c) -> p q w c", q=2, w=2)
                    masked(MtRb[:, 2 * j:2 * j + 2, 0, :], src[:, :, 0, :], level[:, 0, :], 2)
                    masked(MtRb[:, 2 * j:2 * j + 2, 1, :], src[:, :, 1, :], up_incl[:, kind, :], 2).then_inc(S["gram_b_taken"], 1)
                dve.wait_ge(S["gram_b_taken"], 4 * t + 4)
                tt(MtRb[:, :, 0, :], MtRb[:, :, 0, :], ident.unsqueeze(1).to_broadcast([P, H, P]), ALU.add).then_inc(S["g_first"], 1)
                for j in range(2):
                    dve.wait_ge(S["gram_m"], 2 * t + j + 1)
                    ch(masked(Ms[:, 4 * j:4 * j + 4, :], PS[:, j, :].rearrange("p (q c) -> p q c", q=4), low_strict[:, kind, :], 4))
                for j in range(4):
                    dve.wait_ge(S["gram_k"], 4 * t + j + 1)
                    src = PS[:, 4 + j, :].rearrange("p (q w c) -> p q w c", q=2, w=2)
                    masked(NtRk[:, 2 * j:2 * j + 2, 0, :], src[:, :, 0, :], up_strict[:, kind, :], 2)
                    masked(NtRk[:, 2 * j:2 * j + 2, 1, :], src[:, :, 1, :], up_incl[:, kind, :], 2).then_inc(S["gram_k_taken"], 1)
                for l in range(nlev):
                    for grp in range(2):
                        n = 2 * (lev0 + l) + grp
                        qs = slice(4 * grp, 4 * grp + 4)
                        dve.wait_ge(S["r_ready"], n + 1)
                        if l:
                            dve.wait_ge(S["g_ready"], n - 1)
                        masked(Rs[:, qs, :], PS[:, 4 + grp, :].rearrange("p (q c) -> p q c", q=4), level[:, l + 1, :], 4)\
                            .then_inc(S["r_taken"], 1)
                    for grp in range(2):
                        n = 2 * (lev0 + l) + grp
                        qs = slice(4 * grp, 4 * grp + 4)
                        dve.wait_ge(S["g_ready"], n + 1)
                        dve.wait_ge(S["g_first"], t + 1)
                        tt(MtRb[:, qs, 0, :], PS[:, 6 + grp, :].rearrange("p (q c) -> p q c", q=4), MtRb[:, qs, 0, :], ALU.add)\
                            .then_inc(S["g_added"], 1)
                if t == 1:
                    dve.wait_ge(S["ln_in"], 48)
                    lns = Ln.rearrange("p t (k h) -> p t h k", h=H)
                    for t2 in range(2):
                        for h in range(H):
                            ins = v.tensor_tensor_scan(Rt[:, t2, h], ones, lns[:, t2, h], 0.0, ALU.mult, ALU.add)
                    ins.then_inc(S["tot_ready"], 1)
                for c in range(1 if t == 0 else 2):
                    n = ch0 + c
                    rows = slice(64 * c, 64 * c + 64)
                    dc = 0 if t == 0 else 1 + DB + n - 1
                    dve.wait_ge(S["u_ready"], n + 1)
                    v.tensor_copy(Us[rows], PS[rows, 2, :]).then_inc(S["u_taken"], 1)
                    dve.wait_ge(S["st_ready"], n + 1)
                    for hp in range(2):
                        lo = slice(64 * hp, 64 * hp + 64)
                        src = PS[lo, 4, 0:NG * HD].rearrange("p (g i) -> p g i", g=NG)
                        ch(tt(tmpS[lo], src, ST[lo, :, lo], ALU.add))
                    ch.wait()
                    for hp in range(2):
                        lo = slice(64 * hp, 64 * hp + 64)
                        ins = tt(ST[lo, :, lo], tmpS[lo], Dc[lo, :, dc:dc + 1].to_broadcast([64, NG, HD]), ALU.mult)
                    ins.then_inc(S["st_done"], 1)
                    dve.wait_ge(S["st_done"], n + 2)
                if t == 2:
                    dve.wait_ge(S["later_sum"], 1)
                    dve.wait_ge(S["tot_ready"], 1)
                    tt(Rt.rearrange("p t h k -> p (t h) k"), PS[:, 7, 0:2 * H].unsqueeze(2).to_broadcast([P, 2 * H, PAGE]),
                       Rt.rearrange("p t h k -> p (t h) k"), ALU.subtract).then_inc(S["rt_ready"], 1)
                if t == 0:
                    dve.wait_ge(S["us_ready"], 1)
                    v.tensor_copy(Us[64:P], PS[64:P, 2, :]).then_inc(S["us_taken"], 1)
                    dve.wait_ge(S["us_taken"], 1)
                    dve.wait_ge(S["y_ready"], 1)
                    for h in range(H):
                        g = h // 2
                        if h:
                            dve.wait_ge(S["sn_ready"], h)
                        for w, src in enumerate((Us, nat_[:, 3, :])):
                            s_ = src[64:P, h * HD:(h + 1) * HD].unsqueeze(1).to_broadcast([64, DB, HD])
                            ins = tt(Um[64:P, w], s_, seq_of[64:P].unsqueeze(2).to_broadcast([64, DB, HD]), ALU.mult)
                        ins.then_inc(S["um_ready"], 1)
                        if h % 2 == 0:
                            continue
                        dve.wait_ge(S["sn_ready"], h + 1)
                        for hp in range(2):
                            lo = slice(64 * hp, 64 * hp + 64)
                            ch(tt(Sn[lo, g, :].rearrange("p (b i) -> p b i", b=DB),
                                  PS[lo, 6 + g % 2, :].rearrange("p (b i) -> p b i", b=DB), S0T[lo, :, g, lo], ALU.add))
                        ch.wait()
                        sg = Sn[:, g, :].rearrange("p (b i) -> p b i", b=DB)
                        tt(sg, sg, Dc[:, g, 1:1 + DB].unsqueeze(2).to_broadcast([P, DB, HD]), ALU.mult).then_inc(S["sn_taken"], 1)
                    v.memset(small[:, 2:3], 0.0).then_inc(S["um_used"], H)
                v.memset(small[:, 3:4], 0.0).then_inc(S["prev_tile"], 1)
                dve.wait_ge(S["prev_tile"], t + 1)

            dve.wait_ge(S["y_taken"], NTILE)
            v.memset(small[:, 5:6], 0.0).then_inc(S["k_free"], NRING)
            v.memset(small[:, 0:1], 0.0).then_inc(S["hs_in"], 1)
            for g in range(NG):
                n = 2 * NG + g
                dve.wait_ge(S["hs_ready"], n + 1)
                ins = stt(two(YT[:, g]), hs(n), -1.0 / HD, two(YT[:, g]), ALU.mult, ALU.add).then_inc(S["hs_taken"], 1)
            dve.wait_ge(S["hs_taken"], 3 * NG)
            v.memset(small[:, 1:2], 0.0).then_inc(S["yc_ready"], 1)
            dve.wait_ge(S["hs_rows"], 2)
            ts(two(Rn), PS[:, 0:2, 0:HT], 1.0 / HD, GN_EPS, ALU.mult, ALU.add).then_inc(S["root_in"], 1)
            dve.wait_ge(S["root_done"], 2)
            v.reciprocal(Rn, Rn).then_inc(S["hs_in"], 1)
            for g in range(NG):
                n = 3 * NG + g
                dve.wait_ge(S["hs_ready"], n + 1)
                stt(two(YT[:, g]), two(YT[:, g]), pc("gn_g", g), hs(n), ALU.mult, ALU.mult).then_inc(S["hs_taken"], 1)
            dve.wait_ge(S["hs_taken"], 4 * NG)
            for g in range(NG):
                ch(stt(YT[:, g], YT[:, g], pc("gn_b", g), kk[:, g], ALU.add, ALU.add))
            ch.wait()
            tt(mixT[:, NG:, 0:SEQ], YT[:, :, P:TL], gate[:, :, P:TL], ALU.mult)
            tt(mixT[:, NG:, SEQ:OUTC], YT[:, :, 64:P], gate[:, :, 64:P], ALU.mult).then_inc(S["rwkv_done"], 1)
            dve.wait_ge(S["rwkv_done"], 1)

            ch(v.memset(RNp, 0.0))
            ch(v.memset(Qc, 0.0))
            ch.wait()
            v.tensor_copy(RNp[:, :, :, 0:2 * DS], RN.rearrange("p b h t -> p b (h t)").rearrange("p b (g n) -> p b g n", g=NG))\
                .then_inc(S["rn_padded"], 1)
            ch(v.memset(Rr, 0.0))
            ch.wait()
            v.memset(small[:, 6:7], 0.0).then_inc(S["v_free"], NRING)

            def take_probs(b, j):
                dve.wait_ge(S["pr_turned"], b * NLOT + (j + 1))
                v.tensor_copy(PTs[:, j % 2], PS[:, 5 + j % 2, :].rearrange("p (a n) -> p a n", a=LOT)).then_inc(S["pr_taken"], 1)

            def take_new_probs(b):
                dve.wait_ge(S["prn_turned"], b + 1)
                v.tensor_copy(PTn, PS[:, 7, P:2 * P]).then_inc(S["prn_taken"], 1)

            def take_scores(b, j, prev):
                dve.wait_ge(S["sc_page"], b * NPG + LOT * (j + 1))
                dve.wait_ge(S[f"r_in{2 * j // NLOT}"], 16 * H * (b + 1))
                if prev:
                    dve.wait_ge(S["exp_out"], (b - 1) * NEXP + (LOT * (j + 1) // 11 + 1))
                blocks = slice(1 + LOT * j, 1 + LOT * (j + 1))
                tt(Sb[:, blocks, :], PS[:, 2 + j % 2, :].rearrange("p (a n) -> p a n", a=LOT), Rr[:, LOT * j:LOT * (j + 1), :],
                   ALU.add).then_inc(S["sc_taken"], 1)
                dve.wait_ge(S["sc_taken"], b * NLOT + (j + 1))
                v.tensor_reduce(mxg[:, 1 + j:2 + j], Sb[:, blocks, :].rearrange("p a n -> p (a n)"), AX.X, ALU.max)\
                    .then_inc(S["mxg_done"], 1)

            def take_new_scores(b):
                dve.wait_ge(S["new_ready"], b + 1)
                tt(Sb[:, 0, :], PS[:, 7, 0:P], RNT[:, bass.ds(b, 1)].rearrange("p o n -> p (o n)"), ALU.add)\
                    .then_inc(S["new_taken"], 1)
                dve.wait_ge(S["new_taken"], b + 1)
                v.tensor_reduce(mxg[:, 0:1], Sb[:, 0, :], AX.X, ALU.max).then_inc(S["mxg_done"], 1)

            def row_sums(b):
                dve.wait_ge(S["exp_out"], (b + 1) * NEXP)
                v.tensor_reduce(rs, ss3, AX.X, ALU.add).then_inc(S["sum_steps"], 1)
                dve.wait_ge(S["sum_steps"], 2 * b + 1)
                v.reciprocal(rden, rs).then_inc(S["sum_steps"], 1)

            def take_output(b):
                dve.wait_ge(S["v_free"], NRING + NPG + b * NPG)
                dve.wait_ge(S["sum_steps"], 2 * b + 2)
                ts(Oc, PS[:, 4, 0:P], rden, None, ALU.mult).then_inc(S["o_scaled"], 1)
                dve.wait_ge(S["o_turned"], b + 1)
                for hp in range(2):
                    lo = slice(64 * hp, 64 * hp + 64)
                    own = PS[lo, 4, P:2 * P].rearrange("p (g n) -> p g n", g=NG)[:, :, DS * hp:DS * hp + DS]
                    ins = v.tensor_copy(mixT[lo, 0:NG, bass.ds(SEQ + b * DS, DS)], own)
                ins.then_inc(S["o_done"], 1)

            def scores_of(b, prev):
                if prev:
                    dve.wait_ge(S["sc_page"], b * NPG)
                v.tensor_copy(Qc[:, :, 0:2 * DS], QB[:, bass.ds(b, 1)].rearrange("p o g n -> p (o g) n")).then_inc(S["qc_ready"], 1)
                for j in range(NLOT):
                    if prev and j == 0:
                        take_new_probs(b - 1)
                    if prev:
                        take_probs(b - 1, j)
                    take_scores(b, j, prev)
                    if j == 1:
                        take_new_scores(b)
                    if prev and j == 2:
                        row_sums(b - 1)
                dve.wait_ge(S["mxg_done"], (b + 1) * (NLOT + 1))
                v.tensor_reduce(m1, mxg, AX.X, ALU.max).then_inc(S["max_steps"], 1)
                dve.wait_ge(S["max_steps"], 2 * b + 1)
                ts(nm, m1, -1.0, None, ALU.mult).then_inc(S["max_steps"], 1)
                if prev:
                    take_output(b - 1)

            scores_of(0, False)
            with dve.Fori(1, DB) as b:
                scores_of(b, True)

            order = [1, 2, 3, 4, 0]

            def rows_of(i):
                return (slice(64, P), slice(SEQ, OUTC)) if i == 0 else (slice(0, P), slice((i - 1) * P, i * P))

            def root(n, i, turn):
                rows, _ = rows_of(i)
                k = (turn + 1) * NTILE + n + 1
                dve.wait_ge(S["square_done"], k)
                ts(rstd[rows, i:i + 1], rstd[rows, i:i + 1], 1.0 / D, RMS_EPS, ALU.mult, ALU.add).then_inc(S["var_done"], 1)
                dve.wait_ge(S["std_done"], k)
                ch(v.reciprocal(rstd[rows, i:i + 1], ss[rows, i:i + 1]))
                ch.wait()

            def add_residual(n):
                i = order[n]
                rows, _ = rows_of(i)
                dve.wait_ge(S["mixed_out"], n + 1)
                dve.wait_ge(x_in[i], 64 if i == 0 else 32)
                xv = x[rows, i, :].rearrange("p (a b) -> p a b", a=2)
                tt(xv, PS[rows, 2 * (n % 2):2 * (n % 2) + 2, :], xv, ALU.add).then_inc(S["h_ready"], 1)

            def norm_rows(m):
                i = order[m]
                rows, _ = rows_of(i)
                root(m, i, 0)
                dve.wait_ge(S["h_ready"], m + 1)
                if m >= 2:
                    dve.wait_ge(S["xT_turned"], NTILE + m - 1)
                ts(xs2[rows, m % 2, :], x[rows, i, :], rstd[rows, i:i + 1], None, ALU.mult).then_inc(S["xs_ready"], 1)

            def take_turned(m):
                rows, cols = rows_of(order[m])
                w = cols.stop - cols.start
                dve.wait_ge(S["xT_turned"], NTILE + m + 1)
                for hf in range(2):
                    gain = par[:, pcol["ln2_g"] + 4 * hf:pcol["ln2_g"] + 4 * hf + 4].unsqueeze(2)
                    src = PS[:, 4 + 2 * (m % 2) + hf, 0:4 * w].rearrange("p (f c) -> p f c", c=w)
                    ins = tt(hT[:, 4 * hf:4 * hf + 4, cols], src, gain.to_broadcast([P, 4, w]), ALU.mult)
                ins.then_inc(S["xnT_ready"], 1)

            take_new_probs(DB - 1)
            for j in range(NLOT):
                take_probs(DB - 1, j)
                if j % 2:
                    add_residual(j // 2)
                    if j in (3, 5):
                        norm_rows(j // 2 - 1)
            row_sums(DB - 1)
            take_output(DB - 1)
            dve.wait_ge(S["o_done"], DB)
            v.memset(small[:, 4:5], 0.0).then_inc(S["attn_done"], 1)
            for m in range(2):
                take_turned(m)
                norm_rows(m + 2)
            add_residual(4)
            take_turned(2)
            norm_rows(4)
            take_turned(3)
            take_turned(4)
            HO = OUTC // 2
            for f in range(NF):
                dve.wait_ge(S["silu_done"], f + 1)
                tt(actT[:, f, :].rearrange("p (a b) -> p a b", a=2), PS[:, 4 * (f % 2) + 2:4 * (f % 2) + 4, 0:HO],
                   sgate[:, f % 2, :].rearrange("p (a b) -> p a b", a=2), ALU.mult).then_inc(S["act_ready"], 1)

            def last_norm(n):
                i = order[n]
                rows, _ = rows_of(i)
                root(n, i, 1)
                dve.wait_ge(S["h_ready"], NTILE + n + 1)
                dve.wait_ge(S["down_taken"], NTILE)
                stt(x[rows, i, :], x[rows, i, :], rstd[rows, i:i + 1], lnf[rows], ALU.mult, ALU.mult).then_inc(S["y_final"], 1)

            dve.wait_ge(S["wo_in"], 32)
            for half in range(2):
                for n, i in enumerate(order):
                    rows, _ = rows_of(i)
                    if n < NTILE - 1:
                        dve.wait_ge(S["down_tile"], (NTILE - 1) * half + n + 1)
                    else:
                        dve.wait_ge(S["down_used"], 3 * (half + 1))
                    xv = x[rows, i, half * NB:(half + 1) * NB]
                    tt(xv, PS[rows, (5 * half + n) % 8, :], xv, ALU.add).then_inc(S["h_ready"] if half else S["down_taken"], 1)
                    if half and n:
                        last_norm(n - 1)
            last_norm(NTILE - 1)

        assert N_OUT_DMA[0] == N_FIRST_OUT + NTILE

        @block.sync
        def _(sp):
            sp.wait_ge(S["out_done"], 16 * N_OUT_DMA[0])
            for n in range(2):
                sp.wait_ge(S[f"so_out{n}"], 64)
            sp.wait_ge(S["fs_out"], 32)


_OUTS = [("y_prompt", (1, SEQ, D)), ("y_sample", (DB, DS, D)), ("k_prompt", (1, 1, NPT, H, HD)), ("v_prompt", (1, 1, NPT, H, HD)),
         ("logf_prompt", (1, 1, NPT, H)), ("wkv_prompt", (1, 1, H, HD, HD)), ("shift_prompt", (1, 1, D)),
         ("k_sample", (1, DB, DS, H, HD)), ("v_sample", (1, DB, DS, H, HD)), ("logf_sample", (1, DB, DS, H)),
         ("wkv_sample", (1, DB, H, HD, HD)), ("shift_sample", (1, DB, D))]


def kernel(**inputs):
    import numpy as _np
    import concourse.bacc as _bacc
    from concourse import mybir as _mybir
    from concourse.bass_utils import run_bass_kernel_spmd as _run

    nc = _bacc.Bacc("TRN2", target_bir_lowering=False, num_devices=1)
    arrays, t_in, t_out = {}, {}, {}
    for name, a in inputs.items():
        a = _np.ascontiguousarray(a)
        arrays[f"in_{name}"] = a
        t_in[name] = nc.dram_tensor(f"in_{name}", a.shape, _mybir.dt.from_np(a.dtype), kind="ExternalInput").ap()
    for name, shape in _OUTS:
        t_out[name] = nc.dram_tensor(f"out_{name}", shape, _mybir.dt.float32, kind="ExternalOutput").ap()
    build(nc, t_in, t_out)
    r = _run(nc, [arrays], core_ids=[0])
    return tuple(r.results[0][f"out_{name}"] for name, _ in _OUTS)
```
